# Optimizing a Trainium2 kernel written in Bass

```python
import jax, jax.numpy as jnp
from jax import lax
import numpy as np

D_MODEL = 1024
BATCH = 1
SEQ = 512
DEPTH = 1

HEAD_DIM = 64
H_FOX = 8
H_DSA = 8
W_FOX = H_FOX * HEAD_DIM
W_DSA = H_DSA * HEAD_DIM
MIX_WIDTH = W_FOX + W_DSA
H_IDX = 8
D_IDX = 64
TOPK_MAX = 256
Q_BLOCK = 128
EPS = 1e-6

IN_WIDTHS = (
    W_FOX, W_FOX, W_FOX,
    H_FOX,
    W_FOX,
    W_DSA, W_DSA, W_DSA,
    H_IDX * D_IDX,
    D_IDX,
    H_IDX,
    W_DSA,
)
N_IN = sum(IN_WIDTHS)
IN_SPLITS = tuple(int(v) for v in np.cumsum(IN_WIDTHS)[:-1])

kernel_name = "hybrid_fox_dsa_adaln_block"

def _rmsnorm(x, gain):
    x32 = x.astype(jnp.float32)
    y = x32 * lax.rsqrt(jnp.mean(x32 * x32, axis=-1, keepdims=True) + EPS)
    return y.astype(x.dtype) * gain

def _to_blocks(a):
    b, s = a.shape[:2]
    return jnp.swapaxes(a.reshape(b, s // Q_BLOCK, Q_BLOCK, *a.shape[2:]), 0, 1)

def _from_blocks(a):
    a = jnp.swapaxes(a, 0, 1)
    return a.reshape(a.shape[0], -1, *a.shape[3:])

def _alibi_slopes(n_heads):
    i = jnp.arange(1, n_heads + 1, dtype=jnp.float32)
    return jnp.exp2(-8.0 * i / n_heads)

def fox_attention(q, k, v, log_f):
    s_len = q.shape[1]
    scale = HEAD_DIM ** -0.5
    cum_f = jnp.cumsum(log_f.astype(jnp.float32), axis=1)
    cum_f_keys = jnp.swapaxes(cum_f, 1, 2)
    pos = jnp.arange(s_len)

    def block(args):
        qb, fq, tq = args
        logits = jnp.einsum('bqhd,bshd->bhqs', qb, k).astype(jnp.float32) * scale
        logits = logits + (jnp.swapaxes(fq, 1, 2)[..., :, None] - cum_f_keys[..., None, :])
        causal = pos[None, :] <= tq[:, None]
        logits = jnp.where(causal[None, None], logits, -jnp.inf)
        p = jax.nn.softmax(logits, axis=-1).astype(v.dtype)
        return jnp.einsum('bhqs,bshd->bqhd', p, v)

    out = lax.map(block, (_to_blocks(q), _to_blocks(cum_f), pos.reshape(-1, Q_BLOCK)))
    return _from_blocks(out)

def dsa_attention(q, k, v, q_idx, k_idx, w_idx):
    s_len = q.shape[1]
    top_k = min(TOPK_MAX, s_len // 4)
    scale = HEAD_DIM ** -0.5
    idx_scale = (D_IDX ** -0.5) * (H_IDX ** -0.5)
    slopes = _alibi_slopes(H_DSA)
    pos = jnp.arange(s_len)
    gather = jax.vmap(lambda arr, ii: arr[ii])

    def block(args):
        qb, qib, wb, tq = args
        s_h = jnp.einsum('bqhi,bsi->bqhs', qib, k_idx).astype(jnp.float32)
        index_score = jnp.einsum('bqh,bqhs->bqs', wb.astype(jnp.float32), jax.nn.relu(s_h)) * idx_scale
        causal = pos[None, :] <= tq[:, None]
        index_score = jnp.where(causal[None], index_score, -jnp.inf)
        _, sel = lax.top_k(index_score, top_k)
        k_sel = gather(k, sel)
        v_sel = gather(v, sel)
        logits = jnp.einsum('bqhd,bqkhd->bhqk', qb, k_sel).astype(jnp.float32) * scale
        dist = (tq[None, :, None] - sel).astype(jnp.float32)
        logits = logits - slopes[None, :, None, None] * dist[:, None]
        valid = sel <= tq[None, :, None]
        logits = jnp.where(valid[:, None], logits, -jnp.inf)
        p = jax.nn.softmax(logits, axis=-1).astype(v.dtype)
        return jnp.einsum('bhqk,bqkhd->bqhd', p, v_sel)

    out = lax.map(block, (_to_blocks(q), _to_blocks(q_idx), _to_blocks(w_idx),
                          pos.reshape(-1, Q_BLOCK)))
    return _from_blocks(out)

def setup_inputs(seed: int = 0) -> dict:
    key = jax.random.key(seed)
    ks = jax.random.split(key, 10)
    f32 = jnp.float32
    x = jax.random.normal(ks[0], (BATCH, SEQ, D_MODEL), f32)
    c = jax.random.normal(ks[1], (BATCH, D_MODEL), f32)
    w_mod = jax.random.normal(ks[2], (DEPTH, D_MODEL, 3 * D_MODEL), f32) * (0.5 * D_MODEL ** -0.5)
    b_mod = jax.random.normal(ks[3], (DEPTH, 3 * D_MODEL), f32) * 0.02
    norm_gain = 1.0 + 0.05 * jax.random.normal(ks[4], (DEPTH, D_MODEL), f32)
    w_in = jax.random.normal(ks[5], (DEPTH, D_MODEL, N_IN), f32) * (D_MODEL ** -0.5)
    b_forget = jax.random.normal(ks[6], (DEPTH, H_FOX), f32) * 0.1
    w_out = jax.random.normal(ks[7], (DEPTH, MIX_WIDTH, D_MODEL), f32) * (MIX_WIDTH ** -0.5)
    final_gain = 1.0 + 0.05 * jax.random.normal(ks[8], (D_MODEL,), f32)
    return {"x": x, "c": c, "w_mod": w_mod, "b_mod": b_mod, "norm_gain": norm_gain,
            "w_in": w_in, "b_forget": b_forget, "w_out": w_out, "final_gain": final_gain}

def reference(x, c, w_mod, b_mod, norm_gain, w_in, b_forget, w_out, final_gain):
    b, s, _ = x.shape
    c_act = jax.nn.silu(c)
    for layer in range(DEPTH):
        mod = c_act @ w_mod[layer] + b_mod[layer]
        shift, scale, gate = jnp.split(mod, 3, axis=-1)
        h = _rmsnorm(x, norm_gain[layer]) * (1.0 + scale[:, None, :]) + shift[:, None, :]

        proj = h @ w_in[layer]
        (q_a, k_a, v_a, f_logit, g_a,
         q_b, k_b, v_b, q_i, k_i, w_i, g_b) = jnp.split(proj, IN_SPLITS, axis=-1)

        log_f = jax.nn.log_sigmoid((f_logit + b_forget[layer]).astype(jnp.float32))
        y_a = fox_attention(q_a.reshape(b, s, H_FOX, HEAD_DIM),
                            k_a.reshape(b, s, H_FOX, HEAD_DIM),
                            v_a.reshape(b, s, H_FOX, HEAD_DIM), log_f).reshape(b, s, W_FOX)
        y_a = y_a * jax.nn.silu(g_a)

        y_b = dsa_attention(q_b.reshape(b, s, H_DSA, HEAD_DIM),
                            k_b.reshape(b, s, H_DSA, HEAD_DIM),
                            v_b.reshape(b, s, H_DSA, HEAD_DIM),
                            q_i.reshape(b, s, H_IDX, D_IDX), k_i, w_i).reshape(b, s, W_DSA)
        y_b = y_b * jax.nn.silu(g_b)

        y = jnp.concatenate([y_a, y_b], axis=-1) @ w_out[layer]
        x = x + gate[:, None, :] * y
    return _rmsnorm(x, final_gain)


_drawn_inputs = setup_inputs


def setup_inputs(seed=0):
    import zlib

    import numpy as np

    out = dict(_drawn_inputs(seed))
    spreads = {}
    factors = {'b_mod': 3.366, 'norm_gain': 2.771, 'b_forget': 8.0}
    for name, (base, spread) in spreads.items():
        noise = np.random.default_rng([zlib.crc32(name.encode()), seed]).standard_normal(out[name].shape)
        drawn = base * np.exp(spread * noise) if base else spread * noise
        out[name] = __import__('jax').numpy.asarray(drawn.astype(out[name].dtype))
    for name, factor in factors.items():
        out[name] = (out[name] * factor).astype(out[name].dtype)
    return out
```

```python
from contextlib import ExitStack

import numpy as np

import concourse.bass as bass
from concourse import mybir

ALU = mybir.AluOpType
ACT = mybir.ActivationFunctionType
F32 = mybir.dt.float32
F32R = mybir.dt.float32r

P = 128
D_MODEL = 1024
SEQ = 512
HEAD = 64
N_HEAD = 16
N_FOX = 8
N_IDX = 8
TOPK = min(256, SEQ // 4)
EPS = 1e-6
KC = D_MODEL // P
QT = SEQ // P
PAIRS = N_HEAD // 2
T_QIDX = 1
T_PAIR = 5
N_TILES = T_PAIR + 4 * PAIRS
N_WO = 8
HALF = D_MODEL // 2
FOLD = 64
FROW = 96
BIG = 1.0e30
LOW = -3.0e38
TAKEN = -3.4e38
ROUNDS = TOPK // 8
IDX_SCALE = HEAD ** -0.5 * N_IDX ** -0.5
LAST_TILE_N = 2 * P

W_STAGE = 4
MOD_STAGE = 3


def n_keys(i):
    return (i + 1) * P


def n_cols(i):
    return max(LAST_TILE_N, n_keys(i))


def score_at(i):
    return sum(n_keys(j) for j in range(1, i))


def plan_ring():
    return ([("w", t) for t in range(N_TILES)] + [("o", u) for u in range(N_WO // 2)]
            + [("g", c) for c in range(KC)] + [("o", u) for u in range(N_WO // 2, N_WO)])


RING = plan_ring()
RING_AT = {item: e for e, item in enumerate(RING)}


def split_no(item):
    return item[1] if item[0] == "w" else N_TILES + item[1]


def build(nc, small_rows, x, w_mod, b_gate, w_tiles, b_forget, w_out, final_gain, out):
    ctx = ExitStack()
    with ctx:
        plan = {"at": 16512}

        def sb(name, shape, dt=F32, at=None):
            size = 4
            for n in shape[1:]:
                size *= n
            if at is None:
                at = plan["at"]
                plan["at"] += (size + 31) // 32 * 32
            t = nc.alloc_sbuf_tensor_at(name, shape, dt, offset=at)
            return t, at, size

        def sem(name):
            return ctx.enter_context(nc.semaphore(name))

        h_hi, a_hhi, _ = sb("h_hi", [P, KC, SEQ], F32R)
        h_lo, a_hlo, _ = sb("h_lo", [P, KC, SEQ], F32R)
        wo0_hi, _, _ = sb("wo0_hi", [P, PAIRS, HALF], F32R, at=a_hhi)
        wo0_lo, _, _ = sb("wo0_lo", [P, PAIRS, HALF], F32R, at=a_hlo)
        qk, a_qk, _ = sb("qk", [P, 2, 2, 4, SEQ], F32R)
        x_in, _, _ = sb("x_in", [P, QT, D_MODEL], F32, at=a_qk)
        x_norm, _, _ = sb("x_norm", [P, QT, D_MODEL], F32, at=a_qk + 4 * QT * D_MODEL)
        wo1_hi, _, _ = sb("wo1_hi", [P, PAIRS, HALF], F32R, at=a_qk)
        wo1_lo, _, _ = sb("wo1_lo", [P, PAIRS, HALF], F32R, at=a_qk + 4 * PAIRS * HALF)
        pt_hi, a_pt, s_pt = sb("pt_hi", [P, 2, QT, SEQ], F32R)
        pt_lo, _, _ = sb("pt_lo", [P, 2, QT, SEQ], F32R)
        mod_acc, _, s1 = sb("mod_acc", [P, 2 * D_MODEL], F32, at=a_pt)
        mod_in, _, _ = sb("mod_in", [P, MOD_STAGE, 2 * D_MODEL], F32, at=a_pt + s1)
        sq_junk2, _, _ = sb("sq_junk2", [P, D_MODEL], F32, at=a_pt)
        ki_hi, a1, s1 = sb("ki_hi", [P, SEQ], F32R, at=a_pt)
        ki_lo, a1, s1 = sb("ki_lo", [P, SEQ], F32R, at=a1 + s1)
        kwf, a1, s1 = sb("kwf", [P, SEQ], F32, at=a1 + s1)
        relu_s, a1, s1 = sb("relu_s", [P, 2, SEQ], F32, at=a1 + s1)
        gz, a1, s1 = sb("gz", [P, SEQ], F32, at=a1 + s1)
        ga, a1, s1 = sb("ga", [P, SEQ], F32, at=a1 + s1)
        ge, a1, s1 = sb("ge", [P, SEQ], F32, at=a1 + s1)
        gl, a1, s1 = sb("gl", [P, SEQ], F32, at=a1 + s1)
        glf, a1, s1 = sb("glf", [P, SEQ], F32, at=a1 + s1)
        gcum, a1, s1 = sb("gcum", [P, SEQ], F32, at=a1 + s1)
        g_one, a1, s1 = sb("g_one", [P, SEQ], F32, at=a1 + s1)
        w_in, _, _ = sb("w_stage", [P, W_STAGE, KC, P], F32)
        w_hi, a_ws, s_ws = sb("w_hi", [P, 2, KC, P], F32R)
        w_lo, _, _ = sb("w_lo", [P, 2, KC, P], F32R)
        res, _, _ = sb("res", [P, QT, D_MODEL], F32, at=a_ws)
        vv, _, _ = sb("vv", [P, QT, 2, P], F32R)
        gg, a_gg, _ = sb("gg", [P, 2, SEQ], F32)
        fgain, _, _ = sb("fgain", [P, D_MODEL], F32, at=a_gg)
        v_t, a_vt, s1 = sb("v_t", [P, SEQ], F32)
        g_th, _, _ = sb("g_th", [P, SEQ], F32)
        gate_acc, _, _ = sb("gate_acc", [P, D_MODEL], F32, at=a_vt)
        y_f, _, _ = sb("y_f", [P, SEQ], F32)
        y_g, _, _ = sb("y_g", [P, SEQ], F32)
        y_bot, _, _ = sb("y_bot", [HEAD, SEQ], F32)
        y_hi, a_yhi, _ = sb("y_hi", [P, PAIRS, SEQ], F32R)
        y_lo, a_ylo, _ = sb("y_lo", [P, PAIRS, SEQ], F32R)
        h_f, _, _ = sb("h_f", [P, KC, SEQ], F32, at=a_yhi)
        q_idx, _, _ = sb("q_idx", [P, N_IDX, SEQ], F32R, at=a_ylo)
        l_neg, a_l, _ = sb("l_neg", [P, 2, SEQ], F32)
        gate_sb, _, _ = sb("gate_sb", [P, D_MODEL], F32, at=a_l)
        probs, a_p, _ = sb("probs", [P, 3, SEQ], F32)
        o_tmp, _, _ = sb("o_tmp", [P, 2, SEQ], F32, at=a_p)
        sq_junk, _, _ = sb("sq_junk", [P, D_MODEL], F32, at=a_p)
        bias_t, _, _ = sb("bias_t", [P, SEQ], F32R)
        tri, _, _ = sb("tri", [P, SEQ], F32)
        score, _, _ = sb("score", [P, score_at(QT)], F32)
        ident, _, _ = sb("ident", [P, P], F32)
        ones, _, _ = sb("ones", [P, P], F32)
        rows, _, _ = sb("rows", [40, P], F32)
        cols, _, _ = sb("cols", [P, 40], F32)
        c_th, _, _ = sb("c_th", [P, KC], F32)
        c_act, _, _ = sb("c_act", [P, KC], F32)
        mod_sh, _, _ = sb("mod_sh", [P, KC], F32)
        mod_sc, _, _ = sb("mod_sc", [P, KC], F32)
        mod_a, _, _ = sb("mod_a", [P, KC], F32)
        ssq, _, _ = sb("ssq", [P, 2 * QT], F32)
        var, _, _ = sb("var", [P, 2 * QT], F32)
        lnv, _, _ = sb("lnv", [P, 2 * QT], F32)
        r0, _, _ = sb("r0", [P, 2 * QT], F32)
        r1, _, _ = sb("r1", [P, 2 * QT], F32)
        r2, _, _ = sb("r2", [P, 2 * QT], F32)
        r3, _, _ = sb("r3", [P, 2 * QT], F32)
        rstd, _, _ = sb("rstd", [P, 2 * QT], F32)
        w_row, _, _ = sb("w_row", [P, QT, N_IDX], F32)
        bf_col, _, _ = sb("bf_col", [P, 1], F32)
        slope, _, _ = sb("slope", [N_HEAD - N_FOX, 1], F32)
        keyno_i, _, _ = sb("keyno_i", [N_HEAD - N_FOX, SEQ], mybir.dt.int32, at=a_gg)
        l_min, _, _ = sb("l_min", [P, 4], F32)
        p_sum, _, _ = sb("p_sum", [P, 4], F32)
        p_rec, _, _ = sb("p_rec", [P, 4], F32)
        top8, _, _ = sb("top8", [P, 8], F32)
        assert plan["at"] <= 229344, plan["at"]

        bank = [ctx.enter_context(nc.psum_tensor(f"bank{i}", [P, SEQ], F32)) for i in range(8)]
        pj = bank[0:2]
        ps = bank[2:4]
        pt = bank[4:6]
        py, px = bank[6], bank[7]

        s_small = sem("small_loaded")
        s_x = [sem(f"x_loaded{i}") for i in range(QT)]
        s_mod_in = [sem(f"mod_loaded{i}") for i in range(MOD_STAGE)]
        s_bf = sem("b_forget_loaded")
        s_stage = [sem(f"weights_loaded{i}") for i in range(W_STAGE)]
        s_bgate = sem("b_gate_loaded")
        s_res = [sem(f"residual_loaded{i}") for i in range(QT)]
        s_fg = sem("final_gain_loaded")
        s_ident = sem("identity_ready")
        s_const = sem("constants_ready")
        s_rows_t = sem("rows_transposed")
        s_cols = sem("columns_ready")
        s_cth = sem("c_tanh")
        s_cact = sem("c_act_ready")
        s_macc = sem("mod_accumulated")
        s_mred = sem("mod_reduced")
        s_ab = sem("mod_columns_ready")
        s_ssq = sem("square_sums")
        s_var = sem("variances")
        s_ln = sem("log_variances")
        s_r0 = sem("first_rstd")
        s_nw = sem("newton_steps")
        s_xn = sem("x_normalised")
        s_xt = sem("x_transposed")
        s_xe = sem("x_evacuated")
        s_hf = sem("h_ready")
        s_hhi = sem("h_hi_ready")
        s_hlo = sem("h_lo_ready")
        s_whi = sem("weights_hi")
        s_wlo = sem("weights_lo")
        s_proj = sem("tile_projected")
        s_hi = sem("tile_hi_evacuated")
        s_ev = sem("tile_evacuated")
        s_kwf = sem("tile0_copied")
        s_wt = sem("index_weights_transposed")
        s_wr = sem("index_weights_ready")
        s_fg1 = sem("forget_vector_steps")
        s_fg2 = sem("forget_scalar_steps")
        s_bias = sem("key_bias_ready")
        s_kid = sem("index_keys_doubled")
        s_is = sem("index_products")
        s_ir = sem("index_relu")
        s_ia = sem("index_accumulated")
        s_tk = sem("topk_steps")
        s_dup = [sem(f"pair_operands_doubled{i}") for i in range(2)]
        s_th = sem("g_tanh")
        s_vt = sem("v_transposed")
        s_vhi = sem("v_hi")
        s_vlo = sem("v_lo")
        s_s = sem("logits_ready")
        s_min = sem("logits_masked")
        s_exp = sem("exp_done")
        s_rec = sem("sum_inverted")
        s_pn = sem("probs_scaled")
        s_tr = sem("probs_transposed")
        s_pth = sem("probs_t_hi")
        s_ptl = sem("probs_t_lo")
        s_pv = sem("values_summed")
        s_yb = sem("y_bottom_copied")
        s_ys = sem("y_summed")
        s_yg = sem("y_gated")
        s_yhi = sem("y_hi")
        s_ylo = sem("y_lo")
        s_gz = sem("gate_acc_zeroed")
        s_ga = sem("gate_accumulated")
        s_gb = sem("gate_broadcast")
        s_gs = sem("gate_stored")
        s_o = sem("output_products")
        s_ot = sem("output_gated")
        s_or = sem("residual_added")
        s_sq2 = sem("final_square_sums")
        s_v2 = sem("final_variances")
        s_l2 = sem("final_log_variances")
        s_r02 = sem("final_first_rstd")
        s_nw2 = sem("final_newton_steps")
        s_fin = sem("rows_finished")
        s_out = sem("rows_stored")

        def tile_no(p, c):
            return T_PAIR + 4 * p + c

        def hi_count(t):
            return t + 1 if t < T_PAIR else T_PAIR + 2 * ((t - T_PAIR) // 4) + (t - T_PAIR) % 4 + 1

        IDX_STEPS = [(i, h) for i in range(1, QT) for h in range(N_IDX)]
        PER_M = 4 * KC * 3 // len(IDX_STEPS)
        ROUND_LIST = [(i, r) for i in range(1, QT) for r in range(ROUNDS)]
        ROUND_SLOTS = 4 * 8
        BANK_X = [0, 1, 2, 3, 4, 5, 0, 1]

        def done_tile(p, j):
            return tile_no(p, 3) + j // 2

        def mod_slot_free(k):
            return k - MOD_STAGE + 1

        O_GROUPS = [(hf, i) for hf in range(2) for i in range(QT)]
        O_EARLY = 2

        def wo_parts(hf):
            return (wo0_hi, wo0_lo) if hf == 0 else (wo1_hi, wo1_lo)

        block = ctx.enter_context(nc.Block())

        def pt_copy(act, a, n):
            i, hp = n % 4, (n // 4) % 2
            act.wait_ge(s_tr, n + 1)
            if n // 4 >= 2:
                act.wait_ge(s_pv, n // 4 - 1)
            if n == 0:
                act.wait_ge(s_const, 4 + 8 + 1 + 8 + 4 + 4)
            a.activation(pt_hi[:, hp, 0:i + 1, i * P:(i + 1) * P],
                         pt[n % 2][:, 0:n_keys(i)].rearrange("p (j q) -> p j q", q=P), ACT.Copy).then_inc(s_pth, 1)

        def y_bottom(act, a, hh):
            act.wait_ge(s_pv, hh + 1)
            if hh >= 1:
                act.wait_ge(s_ys, hh)
            a.activation(y_bot[:, :], py[HEAD:P, :], ACT.Copy).then_inc(s_yb, 1)

        def y_top(act, a, p):
            act.wait_ge(s_yg, p + 1)
            a.activation(y_hi[:, p, :], y_g[:, :], ACT.Copy).then_inc(s_yhi, 1)

        @block.sync
        def _(sp):
            sp.dma_start(rows[:, :], small_rows).then_inc(s_small, 16)
            sp.dma_start(bf_col[FROW:FROW + N_FOX, :], b_forget).then_inc(s_bf, 16)
            for k in range(KC):
                if k < QT:
                    sp.dma_start(x_in[:, k, :], x[0, k * P:(k + 1) * P, :]).then_inc(s_x[k], 16)
                if k >= MOD_STAGE:
                    sp.wait_ge(s_macc, mod_slot_free(k))
                sp.dma_start(mod_in[:, k % MOD_STAGE, :], w_mod[0, k * P:(k + 1) * P, 0:2 * D_MODEL])\
                    .then_inc(s_mod_in[k % MOD_STAGE], 16)

            def load(e):
                kind, n = RING[e]
                if e >= W_STAGE:
                    was = RING[e - W_STAGE]
                    if was[0] == "g":
                        sp.wait_ge(s_ga, was[1] + 1)
                    else:
                        sp.wait_ge(s_wlo, split_no(was) + 1)
                slot = w_in[:, e % W_STAGE, :, :]
                if kind == "w":
                    src = w_tiles[n]
                elif kind == "g":
                    src = w_mod[0, n * P:(n + 1) * P, 2 * D_MODEL:3 * D_MODEL]
                    slot = slot.rearrange("p k c -> p (k c)")
                else:
                    hf, u = divmod(n, N_WO // 2)
                    src = w_out[0, 2 * u * P:(2 * u + 2) * P, hf * HALF:(hf + 1) * HALF]\
                        .rearrange("(a p) n -> p a n", p=P)
                    slot = slot.rearrange("p k c -> p (k c)").rearrange("p (a n) -> p a n", a=2)
                sp.dma_start(slot, src).then_inc(s_stage[e % W_STAGE], 16)

            def copy(dst, src):
                return sp.dma_start(dst.bitcast(F32), src.bitcast(F32))

            def double(t):
                if t == 0:
                    sp.wait_ge(s_hi, 1)
                    copy(ki_hi[HEAD:P, :], ki_hi[0:HEAD, :]).then_inc(s_kid, 16)
                    sp.wait_ge(s_ev, 1)
                    copy(ki_lo[HEAD:P, :], ki_lo[0:HEAD, :]).then_inc(s_kid, 16)
                if t < T_PAIR:
                    return
                p, c = divmod(t - T_PAIR, 4)
                if c > 1:
                    return
                sp.wait_ge(s_hi, hi_count(t))
                for hd in range(2):
                    a = qk[:, p % 2, hd, :, :]
                    if c == 0:
                        copy(a[0:HEAD, 1, :], a[0:HEAD, 0, :]).then_inc(s_dup[p % 2], 16)
                    else:
                        copy(a[HEAD:P, 2, :], a[0:HEAD, 2, :]).then_inc(s_dup[p % 2], 16)
                if c == 1:
                    if p == 0:
                        sp.wait_ge(s_bias, 4)
                    if p >= 2:
                        sp.wait_ge(s_s, 8 * (p - 1))
                    for hd in range(2):
                        h = 2 * p + hd
                        top, low = (FROW + h, FOLD + h) if h < N_FOX else (h - N_FOX, 32 + h - N_FOX)
                        a = qk[:, p % 2, hd, 3, :]
                        copy(a[HEAD:HEAD + 1, :], bias_t[top:top + 1, :]).then_inc(s_dup[p % 2], 16)
                        copy(a[HEAD + 1:HEAD + 2, :], bias_t[low:low + 1, :]).then_inc(s_dup[p % 2], 16)

            for e in range(len(RING)):
                if RING[e] == ("g", 0):
                    sp.wait_ge(s_gz, 1)
                    sp.dma_start(gate_acc[0:1, :], b_gate).then_inc(s_bgate, 16)
                    sp.wait_ge(s_proj, N_TILES)
                    for i in range(QT):
                        sp.dma_start(res[:, i, :], x[0, i * P:(i + 1) * P, :]).then_inc(s_res[i], 16)
                load(e)
                if e >= W_STAGE and e - W_STAGE < N_TILES:
                    double(e - W_STAGE)
            sp.wait_ge(s_yg, PAIRS)
            sp.dma_start(fgain[:, :], final_gain.to_broadcast([P, D_MODEL])).then_inc(s_fg, 16)
            for i in range(QT):
                sp.wait_ge(s_fin, i + 1)
                sp.dma_start(out[0, i * P:(i + 1) * P, :], res[:, i, :]).then_inc(s_out, 16)
            sp.wait_ge(s_out, 16 * QT)

        @block.gpsimd
        def _(pool):
            g = nc.gpsimd
            g.memset(ident[:, :], 0.0).then_inc(s_ident, 1)
            g.memset(ones[:, :], 1.0).then_inc(s_const, 1)
            pool.wait_ge(s_ident, 1)
            g.affine_select(out=ident[:, :], in_=ident[:, :], compare_op=ALU.not_equal, fill=1.0, base=0,
                            pattern=[[-1, P]], channel_multiplier=1).then_inc(s_ident, 1)
            g.memset(tri[:, :], 0.0).then_inc(s_const, 1)
            pool.wait_ge(s_const, 2)
            g.affine_select(out=tri[:, SEQ - P:SEQ], in_=tri[:, SEQ - P:SEQ], compare_op=ALU.is_ge, fill=BIG,
                            base=0, pattern=[[-1, P]], channel_multiplier=1).then_inc(s_const, 1)
            g.memset(slope[:, :], 0.0).then_inc(s_const, 1)
            for h in range(N_HEAD - N_FOX):
                pool.wait_ge(s_const, 4 + h)
                g.affine_select(out=slope[:, :], in_=slope[:, :], compare_op=ALU.not_equal,
                                fill=2.0 ** -(8.0 * (h + 1) / (N_HEAD - N_FOX)), base=-h,
                                pattern=[[0, 1]], channel_multiplier=1).then_inc(s_const, 1)
            g.iota(keyno_i[:, :], pattern=[[1, SEQ]], base=0, channel_multiplier=0).then_inc(s_const, 1)
            pool.wait_ge(s_xt, 8)
            for par in range(2):
                for hd in range(2):
                    g.memset(qk[HEAD:P, par, hd, 1, :].bitcast(F32), 0.0).then_inc(s_const, 1)
                    g.memset(qk[HEAD:P, par, hd, 3, :].bitcast(F32), 0.0).then_inc(s_const, 1)
            pool.wait_ge(s_const, 4 + 8 + 1 + 8)
            for par in range(2):
                for hd in range(2):
                    g.memset(qk[HEAD:HEAD + 2, par, hd, 1, :].bitcast(F32), 1.0).then_inc(s_const, 1)
            pool.wait_ge(s_const, 4 + 8 + 1 + 8 + 4)

            def split_lo(item):
                n, e = split_no(item), RING_AT[item]
                pool.wait_ge(s_whi, n + 1)
                src = w_in[:, e % W_STAGE, :, :]
                if item[0] == "w":
                    g.tensor_tensor(w_lo[:, n % 2, :, :], src, w_hi[:, n % 2, :, :].bitcast(F32), ALU.subtract)\
                        .then_inc(s_wlo, 1)
                else:
                    hf, u = divmod(item[1], N_WO // 2)
                    hi, lo = wo_parts(hf)
                    src = src.rearrange("p k c -> p (k c)").rearrange("p (a n) -> p a n", a=2)
                    g.tensor_tensor(lo[:, 2 * u:2 * u + 2, :], src, hi[:, 2 * u:2 * u + 2, :].bitcast(F32),
                                    ALU.subtract).then_inc(s_wlo, 1)

            for t in range(T_PAIR + 5):
                split_lo(("w", t))
            pool.wait_ge(s_ia, len(IDX_STEPS))
            pool.wait_ge(s_bias, 4)
            for par in range(2):
                g.memset(pt_hi[:, par, QT - 1, 2 * P:3 * P].bitcast(F32), 0.0).then_inc(s_const, 1)
                g.memset(pt_lo[:, par, QT - 1, 2 * P:3 * P].bitcast(F32), 0.0).then_inc(s_const, 1)
            for p in range(PAIRS):
                for j in range(8):
                    n, i = 8 * p + j, j % 4
                    pool.wait_ge(s_rec, n + 1)
                    pr = probs[:, n % 3, 0:n_keys(i)]
                    g.tensor_scalar(pr, pr, p_rec[:, n % 4:n % 4 + 1], 1.0, ALU.mult, ALU.mult)\
                        .then_inc(s_pn, 1)
                    if j % 2 == 0 and done_tile(p, j) + 2 < N_TILES:
                        split_lo(("w", done_tile(p, j) + 2))
                    if p == PAIRS - 1 and j < 2:
                        split_lo(("o", 2 * j))
                        split_lo(("o", 2 * j + 1))
                    if p >= 1 and j == 3:
                        pool.wait_ge(s_yhi, p)
                        g.tensor_tensor(y_lo[:, p - 1, :], y_g[:, :], y_hi[:, p - 1, :].bitcast(F32),
                                        ALU.subtract).then_inc(s_ylo, 1)
                    if p == PAIRS - 1 and j == 3:
                        pool.wait_ge(s_ev, N_TILES)
                        pool.wait_ge(s_vt, PAIRS)
                        g.memset(gate_acc[:, :], 0.0).then_inc(s_gz, 1)
            pool.wait_ge(s_yhi, PAIRS)
            g.tensor_tensor(y_lo[:, PAIRS - 1, :], y_g[:, :], y_hi[:, PAIRS - 1, :].bitcast(F32),
                            ALU.subtract).then_inc(s_ylo, 1)
            for u in range(N_WO // 2, N_WO):
                split_lo(("o", u))

        @block.scalar
        def _(act):
            a = nc.scalar
            act.wait_ge(s_cols, 1)
            a.activation(c_th[:, :], cols[:, 0:KC], ACT.Tanh, scale=0.5).then_inc(s_cth, 1)
            for i in range(QT):
                act.wait_ge(s_x[i], 16)
                if i:
                    act.wait_ge(s_ssq, i)
                a.activation(sq_junk[:, :], x_in[:, i, :], ACT.Square, accum_out=ssq[:, i:i + 1]).then_inc(s_ssq, 1)
            act.wait_ge(s_var, 1)
            a.activation(lnv[:, 0:QT], var[:, 0:QT], ACT.Ln).then_inc(s_ln, 1)
            act.wait_ge(s_ln, 1)
            a.activation(r0[:, 0:QT], lnv[:, 0:QT], ACT.Exp, scale=-0.5).then_inc(s_r0, 1)
            act.wait_ge(s_nw, 4)
            for i in range(QT):
                a.activation(x_norm[:, i, :], x_in[:, i, :], ACT.Copy, scale=rstd[:, i:i + 1]).then_inc(s_xn, 1)
            for i in range(QT):
                for gp in range(2):
                    n = 2 * i + gp
                    act.wait_ge(s_xt, n + 1)
                    a.activation(h_f[:, 4 * gp:4 * gp + 4, i * P:(i + 1) * P],
                                 bank[BANK_X[n]][:, :].rearrange("p (k t) -> p k t", k=4), ACT.Copy)\
                        .then_inc(s_xe, 1)

            def split_hi(item):
                n, e = split_no(item), RING_AT[item]
                act.wait_ge(s_stage[e % W_STAGE], 16 * (e // W_STAGE + 1))
                src = w_in[:, e % W_STAGE, :, :]
                if item[0] == "w":
                    if n >= 2:
                        act.wait_ge(s_proj, n - 1)
                    a.activation(w_hi[:, n % 2, :, :], src, ACT.Copy).then_inc(s_whi, 1)
                else:
                    hf, u = divmod(item[1], N_WO // 2)
                    if hf == 0:
                        act.wait_ge(s_proj, N_TILES)
                    else:
                        act.wait_ge(s_s, 8 * PAIRS)
                    src = src.rearrange("p k c -> p (k c)").rearrange("p (a n) -> p a n", a=2)
                    a.activation(wo_parts(hf)[0][:, 2 * u:2 * u + 2, :], src, ACT.Copy).then_inc(s_whi, 1)

            def evac(t):
                src = pj[t % 2]
                if t < T_PAIR:
                    act.wait_ge(s_proj, t + 1)
                    if t == 0:
                        a.activation(kwf[:, :], src[:, :], ACT.Copy).then_inc(s_kwf, 1)
                        a.activation(ki_hi[0:HEAD, :], src[0:HEAD, :], ACT.Copy).then_inc(s_hi, 1)
                        return
                    for hd in range(2):
                        ins = a.activation(q_idx[0:HEAD, 2 * (t - T_QIDX) + hd, :],
                                           src[hd * HEAD:(hd + 1) * HEAD, :], ACT.Copy)
                    ins.then_inc(s_hi, 1)
                    return
                p, c = divmod(t - T_PAIR, 4)
                if c == 2:
                    return
                act.wait_ge(s_proj, t + 1)
                if c == 3:
                    if p:
                        act.wait_ge(s_ev, tile_no(p - 1, 3) + 1)
                    a.activation(g_th[:, :], src[:, :], ACT.Tanh, scale=0.5).then_inc(s_th, 1)
                    return
                if p == 0 and c == 0:
                    act.wait_ge(s_const, 4 + 8 + 1 + 8 + 4)
                if p >= 2:
                    act.wait_ge(s_s, 8 * (p - 1))
                for hd in range(2):
                    ins = a.activation(qk[0:HEAD, p % 2, hd, 2 * c, :], src[hd * HEAD:(hd + 1) * HEAD, :],
                                       ACT.Copy, scale=-(HEAD ** -0.5) if c == 0 else 1.0)
                ins.then_inc(s_hi, 1)

            split_hi(("w", 0))
            for k in range(KC):
                act.wait_ge(s_hf, k + 1)
                a.activation(h_hi[:, k, :], h_f[:, k, :], ACT.Copy).then_inc(s_hhi, 1)
                if k == 0:
                    split_hi(("w", 1))
            for t in range(T_PAIR):
                evac(t)
                split_hi(("w", t + 2))
                if t == 1:
                    act.wait_ge(s_fg1, 1)
                    a.activation(ga[FROW:FROW + N_FOX, :], gz[FROW:FROW + N_FOX, :], ACT.Abs).then_inc(s_fg2, 1)
                    act.wait_ge(s_fg2, 1)
                    a.activation(ge[FROW:FROW + N_FOX, :], ga[FROW:FROW + N_FOX, :], ACT.Exp, scale=-1.0)\
                        .then_inc(s_fg2, 1)
                    act.wait_ge(s_fg2, 2)
                    a.activation(gl[FROW:FROW + N_FOX, :], ge[FROW:FROW + N_FOX, :], ACT.Ln, bias=1.0)\
                        .then_inc(s_fg2, 1)
            for m, (i, h) in enumerate(IDX_STEPS):
                act.wait_ge(s_is, m + 1)
                if m >= 2:
                    act.wait_ge(s_ia, m - 1)
                a.activation(relu_s[:, m % 2, 0:n_keys(i)], ps[m % 2][:, 0:n_keys(i)], ACT.Relu).then_inc(s_ir, 1)
                if m % 6 == 1 and m > 6:
                    split_hi(("w", tile_no(0, m // 6 - 1) + 2))
                    evac(tile_no(0, m // 6 - 1))
            for p in range(PAIRS):
                for j in range(8):
                    n, i = 8 * p + j, j % 4
                    act.wait_ge(s_min, n + 1)
                    if n >= 3:
                        act.wait_ge(s_tr, n - 2)
                    a.activation(probs[:, n % 3, 0:n_keys(i)], l_neg[:, n % 2, 0:n_keys(i)], ACT.Exp,
                                 bias=l_min[:, n % 4:n % 4 + 1], scale=-1.0,
                                 accum_out=p_sum[:, n % 4:n % 4 + 1]).then_inc(s_exp, 1)
                    if n >= 1:
                        pt_copy(act, a, n - 1)
                    if j % 2 == 0 and done_tile(p, j) + 2 < N_TILES:
                        split_hi(("w", done_tile(p, j) + 2))
                    if p == PAIRS - 1 and j < 2:
                        split_hi(("o", 2 * j))
                        split_hi(("o", 2 * j + 1))
                    if j == 0:
                        evac(tile_no(p, 3))
                    if j in (2, 4) and p < PAIRS - 1:
                        evac(tile_no(p + 1, j // 2 - 1))
                    if j == 2 and p >= 1:
                        y_bottom(act, a, 2 * p - 1)
                    if j == 6:
                        y_bottom(act, a, 2 * p)
                    if j == 3:
                        act.wait_ge(s_vt, p + 1)
                        if p >= 1:
                            act.wait_ge(s_pv, 2 * p)
                        a.activation(vv[:, :, :, 0:HEAD],
                                     px[:, :].rearrange("p (j h d) -> p j h d", j=QT, h=2), ACT.Copy)\
                            .then_inc(s_vhi, 1)
                        if p >= 1:
                            y_top(act, a, p - 1)
            pt_copy(act, a, 8 * PAIRS - 1)
            y_bottom(act, a, 2 * PAIRS - 1)
            y_top(act, a, PAIRS - 1)
            for u in range(N_WO // 2, N_WO):
                split_hi(("o", u))
            for i in range(QT):
                act.wait_ge(s_or, QT + i + 1)
                if i:
                    act.wait_ge(s_sq2, i)
                a.activation(sq_junk2[:, :], res[:, i, :], ACT.Square, accum_out=ssq[:, QT + i:QT + i + 1]).then_inc(s_sq2, 1)
                act.wait_ge(s_v2, i + 1)
                a.activation(lnv[:, QT + i:QT + i + 1], var[:, QT + i:QT + i + 1], ACT.Ln).then_inc(s_l2, 1)
                act.wait_ge(s_l2, i + 1)
                a.activation(r0[:, QT + i:QT + i + 1], lnv[:, QT + i:QT + i + 1], ACT.Exp, scale=-0.5)\
                    .then_inc(s_r02, 1)

        @block.vector
        def _(dve):
            v = nc.vector
            dve.wait_ge(s_rows_t, 1)
            v.tensor_copy(cols[:, :], py[:, 0:40]).then_inc(s_cols, 1)
            dve.wait_ge(s_cols, 1)
            dve.wait_ge(s_cth, 1)
            v.tensor_scalar(c_th[:, :], c_th[:, :], 0.5, 0.5, ALU.mult, ALU.add).then_inc(s_cact, 1)
            dve.wait_ge(s_cact, 1)
            v.tensor_tensor(c_act[:, :], c_th[:, :], cols[:, 0:KC], ALU.mult).then_inc(s_cact, 1)
            dve.wait_ge(s_cact, 2)

            def rms(sum_of, cols_, s_sum, n_sum, s_variance, s_first, n_first, s_steps, n_steps):
                dve.wait_ge(s_sum, n_sum)
                v.tensor_scalar(var[:, cols_], ssq[:, cols_], 1.0 / D_MODEL, EPS, ALU.mult, ALU.add)\
                    .then_inc(s_variance, 1)
                dve.wait_ge(s_first, n_first)
                v.tensor_tensor(r1[:, cols_], r0[:, cols_], r0[:, cols_], ALU.mult).then_inc(s_steps, 1)
                dve.wait_ge(s_steps, n_steps + 1)
                v.tensor_tensor(r2[:, cols_], r1[:, cols_], var[:, cols_], ALU.mult).then_inc(s_steps, 1)
                dve.wait_ge(s_steps, n_steps + 2)
                v.tensor_scalar(r3[:, cols_], r2[:, cols_], -0.5, 1.5, ALU.mult, ALU.add).then_inc(s_steps, 1)
                dve.wait_ge(s_steps, n_steps + 3)
                v.tensor_tensor(rstd[:, cols_], r3[:, cols_], r0[:, cols_], ALU.mult).then_inc(s_steps, 1)

            for k in range(KC):
                dve.wait_ge(s_mod_in[k % MOD_STAGE], 16 * (k // MOD_STAGE + 1))
                if k:
                    dve.wait_ge(s_macc, k)
                if k == 0:
                    v.tensor_scalar(mod_acc[:, :], mod_in[:, 0, :], c_act[:, 0:1], None, ALU.mult).then_inc(s_macc, 1)
                else:
                    v.scalar_tensor_tensor(out=mod_acc[:, :], in0=mod_in[:, k % MOD_STAGE, :],
                                           scalar=c_act[:, k:k + 1], in1=mod_acc[:, :],
                                           op0=ALU.mult, op1=ALU.add).then_inc(s_macc, 1)
                if k == 4:
                    rms("x", slice(0, QT), s_ssq, QT, s_var, s_r0, 1, s_nw, 0)
            dve.wait_ge(s_mred, 1)
            v.tensor_tensor(mod_sh[:, :], px[:, 0:KC], cols[:, 2 * KC:3 * KC], ALU.add).then_inc(s_ab, 1)
            v.tensor_tensor(mod_sc[:, :], px[:, KC:2 * KC], cols[:, 3 * KC:4 * KC], ALU.add).then_inc(s_ab, 1)
            dve.wait_ge(s_ab, 2)
            v.scalar_tensor_tensor(out=mod_a[:, :], in0=mod_sc[:, :], scalar=1.0, in1=cols[:, KC:2 * KC],
                                   op0=ALU.add, op1=ALU.mult).then_inc(s_ab, 1)
            dve.wait_ge(s_ab, 3)
            dve.wait_ge(s_xe, 2 * QT)
            for k in range(KC):
                v.tensor_scalar(h_f[:, k, :], h_f[:, k, :], mod_a[:, k:k + 1], mod_sh[:, k:k + 1],
                                ALU.mult, ALU.add).then_inc(s_hf, 1)
                if k:
                    dve.wait_ge(s_hhi, k)
                    v.tensor_tensor(h_lo[:, k - 1, :], h_f[:, k - 1, :], h_hi[:, k - 1, :].bitcast(F32),
                                    ALU.subtract).then_inc(s_hlo, 1)
            dve.wait_ge(s_hhi, KC)
            v.tensor_tensor(h_lo[:, KC - 1, :], h_f[:, KC - 1, :], h_hi[:, KC - 1, :].bitcast(F32),
                            ALU.subtract).then_inc(s_hlo, 1)
            dve.wait_ge(s_const, 4 + 8 + 1)
            v.tensor_scalar(bias_t[0:N_HEAD - N_FOX, :], keyno_i[:, :], slope[:, 0:1], -1.0, ALU.mult, ALU.mult)\
                .then_inc(s_bias, 1)
            v.memset(bias_t[32:32 + N_HEAD - N_FOX, :].bitcast(F32), 0.0).then_inc(s_bias, 1)

            def evac(t):
                src = pj[t % 2]
                if t < T_PAIR:
                    dve.wait_ge(s_hi, hi_count(t))
                    if t == 0:
                        v.tensor_tensor(ki_lo[0:HEAD, :], src[0:HEAD, :], ki_hi[0:HEAD, :].bitcast(F32),
                                        ALU.subtract).then_inc(s_ev, 1)
                        return
                    for hd in range(2):
                        q = q_idx[:, 2 * (t - T_QIDX) + hd, :]
                        ins = v.tensor_tensor(q[HEAD:P, :], src[hd * HEAD:(hd + 1) * HEAD, :],
                                              q[0:HEAD, :].bitcast(F32), ALU.subtract)
                    ins.then_inc(s_ev, 1)
                    return
                p, c = divmod(t - T_PAIR, 4)
                if c == 2:
                    dve.wait_ge(s_proj, t + 1)
                    if p:
                        dve.wait_ge(s_vt, p)
                    v.tensor_copy(v_t[:, :], src[:, :]).then_inc(s_ev, 1)
                    return
                if c == 3:
                    dve.wait_ge(s_th, p + 1)
                    if p >= 2:
                        dve.wait_ge(s_yg, p - 1)
                    v.scalar_tensor_tensor(out=gg[:, p % 2, :], in0=g_th[:, :], scalar=1.0, in1=src[:, :],
                                           op0=ALU.add, op1=ALU.mult).then_inc(s_ev, 1)
                    return
                dve.wait_ge(s_hi, hi_count(t))
                for hd in range(2):
                    o = qk[:, p % 2, hd, :, :]
                    part = src[hd * HEAD:(hd + 1) * HEAD, :]
                    if c == 0:
                        ins = v.scalar_tensor_tensor(out=o[HEAD:P, 0, :], in0=part, scalar=-(HEAD ** -0.5),
                                                     in1=o[0:HEAD, 0, :].bitcast(F32),
                                                     op0=ALU.mult, op1=ALU.subtract)
                    else:
                        ins = v.tensor_tensor(o[0:HEAD, 3, :], part, o[0:HEAD, 2, :].bitcast(F32), ALU.subtract)
                ins.then_inc(s_ev, 1)

            F = slice(FROW, FROW + N_FOX)
            for t in range(T_PAIR):
                evac(t)
                if t == 0:
                    dve.wait_ge(s_kwf, 1)
                    dve.wait_ge(s_bf, 16)
                    v.tensor_scalar(gz[F, :], kwf[F, :], bf_col[F, 0:1], None, ALU.add).then_inc(s_fg1, 1)
                if t == 2:
                    dve.wait_ge(s_fg2, 3)
                    v.scalar_tensor_tensor(out=glf[F, :], in0=gz[F, :], scalar=0.0, in1=gl[F, :],
                                           op0=ALU.min, op1=ALU.subtract).then_inc(s_fg1, 1)
                    v.memset(g_one[F, :], 1.0).then_inc(s_fg1, 1)
                    dve.wait_ge(s_fg1, 3)
                    v.tensor_tensor_scan(gcum[F, :], g_one[F, :], glf[F, :], 0.0, ALU.mult, ALU.add)\
                        .then_inc(s_fg1, 1)
                    dve.wait_ge(s_fg1, 4)
                    v.tensor_copy(bias_t[F, :], gcum[F, :]).then_inc(s_bias, 1)
                    dve.wait_ge(s_bias, 3)
                    v.tensor_tensor(bias_t[FOLD:FOLD + N_FOX, :], gcum[F, :], bias_t[F, :].bitcast(F32),
                                    ALU.subtract).then_inc(s_bias, 1)
                if t == 3:
                    dve.wait_ge(s_wt, 1)
                    v.tensor_scalar(w_row[:, :, :],
                                    px[:, :].rearrange("p (i f) -> p i f", i=QT)[:, :, FOLD:FOLD + N_IDX],
                                    IDX_SCALE, None, ALU.mult).then_inc(s_wr, 1)
                    dve.wait_ge(s_wr, 1)
            for m, (i, h) in enumerate(IDX_STEPS):
                sc = score[:, score_at(i):score_at(i) + n_keys(i)]
                dve.wait_ge(s_ir, m + 1)
                rl = relu_s[:, m % 2, 0:n_keys(i)]
                if h == 0:
                    v.tensor_scalar(sc, rl, w_row[:, i, 0:1], None, ALU.mult).then_inc(s_ia, 1)
                else:
                    dve.wait_ge(s_ia, m)
                    v.scalar_tensor_tensor(out=sc, in0=rl, scalar=w_row[:, i, h:h + 1], in1=sc,
                                           op0=ALU.mult, op1=ALU.add).then_inc(s_ia, 1)
                if h == N_IDX - 1:
                    diag = score[:, score_at(i) + i * P:score_at(i) + n_keys(i)]
                    dve.wait_ge(s_ia, m + 1)
                    v.scalar_tensor_tensor(out=diag, in0=tri[:, SEQ - P:SEQ], scalar=LOW / BIG, in1=diag,
                                           op0=ALU.mult, op1=ALU.add).then_inc(s_tk, 1)
                if m % 6 == 1 and m > 6:
                    evac(tile_no(0, m // 6 - 1))

            tk = [QT - 1]

            def topk_round(i, r):
                sc = score[:, score_at(i):score_at(i) + n_keys(i)]
                dve.wait_ge(s_tk, tk[0])
                v.max(top8[:, :], sc).then_inc(s_tk, 1)
                dve.wait_ge(s_tk, tk[0] + 1)
                v.match_replace(sc, top8[:, :], sc, TAKEN).then_inc(s_tk, 1)
                tk[0] += 2
                if r == ROUNDS - 1:
                    dve.wait_ge(s_tk, tk[0])
                    v.tensor_scalar(sc, sc, (LOW + TAKEN) / 2, BIG, ALU.is_gt, ALU.mult).then_inc(s_tk, 1)
                    tk[0] += 1

            def pt_low(n):
                i, hp = n % 4, (n // 4) % 2
                dve.wait_ge(s_pth, n + 1)
                hi = pt_hi[:, hp, 0:i + 1, i * P:(i + 1) * P].bitcast(F32)
                v.tensor_tensor(pt_lo[:, hp, 0:i + 1, i * P:(i + 1) * P],
                                pt[n % 2][:, 0:n_keys(i)].rearrange("p (j q) -> p j q", q=P), hi,
                                ALU.subtract).then_inc(s_ptl, 1)

            def y_sum(hh):
                dve.wait_ge(s_yb, hh + 1)
                if hh >= 2 and hh % 2 == 0:
                    dve.wait_ge(s_yg, hh // 2)
                v.tensor_tensor(y_f[hh % 2 * HEAD:(hh % 2 + 1) * HEAD, :], py[0:HEAD, :], y_bot[:, :], ALU.add)\
                    .then_inc(s_ys, 1)

            def y_gate(p):
                dve.wait_ge(s_ys, 2 * p + 2)
                if p:
                    dve.wait_ge(s_ylo, p)
                v.scalar_tensor_tensor(out=y_g[:, :], in0=y_f[:, :], scalar=0.5, in1=gg[:, p % 2, :],
                                       op0=ALU.mult, op1=ALU.mult).then_inc(s_yg, 1)

            def gate_sum(c):
                e = RING_AT[("g", c)]
                dve.wait_ge(s_stage[e % W_STAGE], 16 * (e // W_STAGE + 1))
                if c == 0:
                    dve.wait_ge(s_bgate, 16)
                if c:
                    dve.wait_ge(s_ga, c)
                v.scalar_tensor_tensor(out=gate_acc[:, :],
                                       in0=w_in[:, e % W_STAGE, :, :].rearrange("p k c -> p (k c)"),
                                       scalar=c_act[:, c:c + 1], in1=gate_acc[:, :],
                                       op0=ALU.mult, op1=ALU.add).then_inc(s_ga, 1)

            done = 0
            for p in range(PAIRS):
                for j in range(8):
                    n, i = 8 * p + j, j % 4
                    dve.wait_ge(s_s, n + 1)
                    if n >= 2:
                        dve.wait_ge(s_exp, n - 1)
                    if n == 4 * N_FOX:
                        dve.wait_ge(s_tk, tk[0])
                    if p < PAIRS // 2 or i == 0:
                        mask = tri[:, SEQ - n_keys(i):SEQ]
                    else:
                        mask = score[:, score_at(i):score_at(i) + n_keys(i)]
                    v.tensor_tensor_reduce(l_neg[:, n % 2, 0:n_keys(i)], ps[n % 2][:, 0:n_keys(i)], mask,
                                           1.0, 3.0e38, ALU.add, ALU.min, l_min[:, n % 4:n % 4 + 1])\
                        .then_inc(s_min, 1)
                    if j == 0:
                        evac(tile_no(p, 3))
                    dve.wait_ge(s_exp, n + 1)
                    v.reciprocal(p_rec[:, n % 4:n % 4 + 1], p_sum[:, n % 4:n % 4 + 1]).then_inc(s_rec, 1)
                    if n >= 1:
                        pt_low(n - 1)
                    if j in (2, 4, 6) and p < PAIRS - 1:
                        evac(tile_no(p + 1, j // 2 - 1))
                    if j == 2 and p >= 1:
                        y_sum(2 * p - 1)
                        y_gate(p - 1)
                    if j == 6:
                        y_sum(2 * p)
                    if j == 3:
                        dve.wait_ge(s_vhi, p + 1)
                        v.tensor_tensor(vv[:, :, :, HEAD:P],
                                        px[:, :].rearrange("p (j h d) -> p j h d", j=QT, h=2),
                                        vv[:, :, :, 0:HEAD].bitcast(F32), ALU.subtract).then_inc(s_vlo, 1)
                    if n < ROUND_SLOTS:
                        upto = len(ROUND_LIST) * (n + 1) // ROUND_SLOTS
                        for i2, r in ROUND_LIST[done:upto]:
                            topk_round(i2, r)
                        done = upto
                    if p == PAIRS - 1 and j >= 4:
                        gate_sum(2 * (j - 4))
                        gate_sum(2 * (j - 4) + 1)
            pt_low(8 * PAIRS - 1)
            y_sum(2 * PAIRS - 1)
            y_gate(PAIRS - 1)
            for hf in range(2):
                dve.wait_ge(s_gb, hf + 1)
                if hf == 0:
                    dve.wait_ge(s_exp, 8 * PAIRS)
                v.tensor_copy(gate_sb[:, hf * HALF:(hf + 1) * HALF], pt[hf][:, :]).then_inc(s_gs, 1)
            dve.wait_ge(s_gs, 2)
            dve.wait_ge(s_fg, 16)
            for n, (hf, i) in enumerate(O_GROUPS):
                dve.wait_ge(s_o, n + 1)
                if n >= 2:
                    dve.wait_ge(s_or, n - 1)
                if n == 0:
                    dve.wait_ge(s_tr, 8 * PAIRS)
                v.tensor_tensor(o_tmp[:, n % 2, :], bank[n][:, :], gate_sb[:, hf * HALF:(hf + 1) * HALF], ALU.mult)\
                    .then_inc(s_ot, 1)
                dve.wait_ge(s_ot, n + 1)
                if hf == 0:
                    dve.wait_ge(s_res[i], 16)
                r = res[:, i, hf * HALF:(hf + 1) * HALF]
                v.tensor_tensor(r, r, o_tmp[:, n % 2, :], ALU.add).then_inc(s_or, 1)
                if hf == 1:
                    rms("res", slice(QT + i, QT + i + 1), s_sq2, i + 1, s_v2, s_r02, i + 1, s_nw2, 4 * i)
                    dve.wait_ge(s_nw2, 4 * i + 4)
                    v.scalar_tensor_tensor(out=res[:, i, :], in0=res[:, i, :], scalar=rstd[:, QT + i:QT + i + 1],
                                           in1=fgain[:, :], op0=ALU.mult, op1=ALU.mult).then_inc(s_fin, 1)

        @block.tensor
        def _(pe):
            t_ = nc.tensor
            pe.wait_ge(s_small, 16)
            pe.wait_ge(s_ident, 2)
            t_.transpose(py[:, 0:40], rows[:, :], ident[0:40, 0:40]).then_inc(s_rows_t, 1)
            for i in range(QT):
                pe.wait_ge(s_xn, i + 1)
                for gp in range(2):
                    n = 2 * i + gp
                    if n >= 6:
                        pe.wait_ge(s_xe, n - 5)
                    for k in range(4):
                        ins = t_.transpose(bank[BANK_X[n]][:, k * P:(k + 1) * P],
                                           x_norm[:, i, (4 * gp + k) * P:(4 * gp + k + 1) * P], ident[:, :])
                    ins.then_inc(s_xt, 1)
            pe.wait_ge(s_macc, KC)
            pe.wait_ge(s_const, 1)
            for cidx in range(2 * KC):
                ins = t_.matmul(px[:, cidx:cidx + 1], mod_acc[:, cidx * P:(cidx + 1) * P], ones[:, 0:1],
                                start=True, stop=True)
            ins.then_inc(s_mred, 1)
            pe.wait_ge(s_xe, 2 * QT)

            def project(t, part, parts):
                steps = [(k, s) for k in range(KC) for s in range(3)]
                size = len(steps) // parts
                acc = pj[t % 2]
                if part == 0:
                    pe.wait_ge(s_wlo, t + 1)
                    if t >= 2:
                        pe.wait_ge(s_ev, t - 1)
                for k, s in steps[part * size:(part + 1) * size]:
                    w = w_lo if s == 0 else w_hi
                    h = h_lo if s == 1 else h_hi
                    if t == 0 and s == 0:
                        pe.wait_ge(s_hlo, k + 1)
                    ins = t_.matmul(acc[:, :], w[:, t % 2, k, :], h[:, k, :],
                                    start=(k == 0 and s == 0), stop=(k == KC - 1 and s == 2))
                if part == parts - 1:
                    ins.then_inc(s_proj, 1)

            for t in range(T_PAIR):
                project(t, 0, 1)
                if t == 1:
                    pe.wait_ge(s_kwf, 1)
                    for i in range(QT):
                        ins = t_.transpose(px[:, i * P:(i + 1) * P], kwf[:, i * P:(i + 1) * P], ident[:, :])
                    ins.then_inc(s_wt, 1)
            for m, (i, h) in enumerate(IDX_STEPS):
                if m == 0:
                    pe.wait_ge(s_kid, 32)
                    pe.wait_ge(s_ev, T_PAIR)
                if m >= 2:
                    pe.wait_ge(s_ir, m - 1)
                q = q_idx[:, h, i * P:(i + 1) * P]
                t_.matmul(ps[m % 2][:, 0:n_keys(i)], q, ki_lo[:, 0:n_keys(i)], start=True, stop=False)
                t_.matmul(ps[m % 2][:, 0:n_keys(i)], q, ki_hi[:, 0:n_keys(i)], start=False, stop=True)\
                    .then_inc(s_is, 1)
                project(tile_no(0, m // 6), m % 6, 6)

            def transposes(n):
                i = n % 4
                pe.wait_ge(s_pn, n + 1)
                if n >= 2:
                    pe.wait_ge(s_ptl, n - 1)
                for j in range(i + 1):
                    ins = t_.transpose(pt[n % 2][:, j * P:(j + 1) * P], probs[:, n % 3, j * P:(j + 1) * P],
                                       ident[:, :])
                ins.then_inc(s_tr, 1)

            def values(hh):
                hp = hh % 2
                pe.wait_ge(s_ptl, 4 * hh + 4)
                pe.wait_ge(s_vlo, hh // 2 + 1)
                if hh:
                    pe.wait_ge(s_ys, hh)
                for j in range(QT):
                    c0 = min(j, QT - 2) * P
                    for src in (pt_lo, pt_hi):
                        ins = t_.matmul(py[:, c0:SEQ], vv[:, j, hp, :], src[:, hp, j, c0:SEQ],
                                        start=(j == 0 and src is pt_lo), stop=(j == QT - 1 and src is pt_hi))
                ins.then_inc(s_pv, 1)

            def out_part(n, pairs):
                hf, i = O_GROUPS[n]
                hi, lo = wo_parts(hf)
                for p in pairs:
                    pe.wait_ge(s_ylo, p + 1)
                    pe.wait_ge(s_wlo, N_TILES + hf * (N_WO // 2) + p // 2 + 1)
                    for s in range(3):
                        y = y_lo if s == 0 else y_hi
                        w = lo if s == 1 else hi
                        ins = t_.matmul(bank[n][:, :], y[:, p, i * P:(i + 1) * P], w[:, p, :],
                                        start=(p == 0 and s == 0), stop=(p == PAIRS - 1 and s == 2))
                    if p == PAIRS - 1:
                        ins.then_inc(s_o, 1)

            for p in range(PAIRS):
                for j in range(8):
                    n, i = 8 * p + j, j % 4
                    if n == 0:
                        pe.wait_ge(s_ir, len(IDX_STEPS))
                    if j == 0:
                        pe.wait_ge(s_dup[p % 2], 128 * (p // 2 + 1))
                        pe.wait_ge(s_ev, tile_no(p, 1) + 1)
                    if n >= 2:
                        pe.wait_ge(s_min, n - 1)
                    a = qk[:, p % 2, j // 4, :, :]
                    t_.matmul(ps[n % 2][:, 0:n_cols(i)], a[0:HEAD + 32, 1, i * P:(i + 1) * P],
                              a[0:HEAD + 32, 3, 0:n_cols(i)], start=True, stop=False)
                    t_.matmul(ps[n % 2][:, 0:n_cols(i)], a[:, 0, i * P:(i + 1) * P],
                              a[:, 2, 0:n_cols(i)], start=False, stop=True).then_inc(s_s, 1)
                    if n >= 1:
                        transposes(n - 1)
                    if j == 1 and p >= 1:
                        values(2 * p - 1)
                    if j == 5:
                        values(2 * p)
                    if j == 2:
                        pe.wait_ge(s_ev, tile_no(p, 2) + 1)
                        if p:
                            pe.wait_ge(s_vlo, p)
                        for b in range(QT):
                            ins = t_.transpose(px[:, b * P:(b + 1) * P], v_t[:, b * P:(b + 1) * P], ident[:, :])
                        ins.then_inc(s_vt, 1)
                    if p < PAIRS - 1:
                        project(tile_no(p + 1, j // 2), j % 2, 2)
                    elif j >= 1:
                        if j == 1:
                            pe.wait_ge(s_ev, N_TILES)
                        for n2 in range(O_EARLY):
                            out_part(n2, [j - 1])
            transposes(8 * PAIRS - 1)
            for n2 in range(O_EARLY, QT):
                if n2 == O_EARLY:
                    pe.wait_ge(s_min, 8 * PAIRS)
                out_part(n2, range(PAIRS - 1))
                if n2 == O_EARLY:
                    values(2 * PAIRS - 1)
            pe.wait_ge(s_ga, KC)
            pe.wait_ge(s_ptl, 8 * PAIRS)
            for hf in range(2):
                t_.matmul(pt[hf][:, :], ones[:, :], gate_acc[:, hf * HALF:(hf + 1) * HALF], start=True, stop=True)\
                    .then_inc(s_gb, 1)
            for n2 in range(QT):
                out_part(n2, [PAIRS - 1])
            pe.wait_ge(s_gs, 2)
            pe.wait_ge(s_ys, 2 * PAIRS)
            for n2 in range(QT, 2 * QT):
                out_part(n2, range(PAIRS))


_SMALL = (2 + 3) * D_MODEL // P


def kernel(x, c, w_mod, b_mod, norm_gain, w_in, b_forget, w_out, final_gain):
    import concourse.bacc as bacc
    from concourse.bass_utils import run_bass_kernel_spmd

    widths = [N_FOX * HEAD] * 3 + [N_FOX, N_FOX * HEAD] + [512] * 3 + [N_IDX * HEAD, HEAD, N_IDX, 512]
    at = np.concatenate([[0], np.cumsum(widths)])
    q_a, k_a, v_a, f_g, g_a, q_b, k_b, v_b, q_i, k_i, w_i, g_b = (slice(at[n], at[n + 1]) for n in range(12))
    w = np.asarray(w_in)[0]
    first = np.zeros((D_MODEL, P), w.dtype)
    first[:, 0:HEAD] = w[:, k_i]
    first[:, FOLD:FOLD + N_IDX] = w[:, w_i]
    first[:, FROW:FROW + N_FOX] = w[:, f_g]
    order = [first] + [w[:, q_i][:, u * P:(u + 1) * P] for u in range(N_IDX // 2)]
    for p in range(PAIRS):
        u = p % (PAIRS // 2)
        for part in ((q_a, k_a, v_a, g_a) if p < PAIRS // 2 else (q_b, k_b, v_b, g_b)):
            order.append(w[:, part][:, u * P:(u + 1) * P])
    w_tiles = np.ascontiguousarray(np.stack(order).reshape(N_TILES, KC, P, P).transpose(0, 2, 1, 3))
    arrays = {
        "small_rows": np.concatenate([np.asarray(a).reshape(-1, P) for a in (c, norm_gain, b_mod)]),
        "x": np.asarray(x), "w_mod": np.asarray(w_mod),
        "b_gate": np.ascontiguousarray(np.asarray(b_mod)[:, 2 * D_MODEL:]),
        "w_tiles": w_tiles, "b_forget": np.asarray(b_forget).reshape(N_FOX, 1),
        "w_out": np.asarray(w_out), "final_gain": np.asarray(final_gain).reshape(1, D_MODEL),
    }
    nc = bacc.Bacc("TRN2", target_bir_lowering=False, num_devices=1)
    args = [nc.dram_tensor(name, a.shape, mybir.dt.from_np(a.dtype), kind="ExternalInput").ap()
            for name, a in arrays.items()]
    out = nc.dram_tensor("out", (1, SEQ, D_MODEL), F32, kind="ExternalOutput").ap()
    build(nc, *args, out)
    r = run_bass_kernel_spmd(nc, [arrays], core_ids=[0])
    return r.results[0]["out"]
```

```python
from contextlib import ExitStack

import numpy as np

import concourse.bass as bass
from concourse import mybir

ALU = mybir.AluOpType
ACT = mybir.ActivationFunctionType
F32 = mybir.dt.float32
F32R = mybir.dt.float32r

P = 128
D_MODEL = 1024
SEQ = 512
HEAD = 64
N_HEAD = 16
N_FOX = 8
N_IDX = 8
TOPK = min(256, SEQ // 4)
EPS = 1e-6
KC = D_MODEL // P
QT = SEQ // P
PAIRS = N_HEAD // 2
T_QIDX = 1
T_PAIR = 5
N_TILES = T_PAIR + 4 * PAIRS
N_WO = 8
HALF = D_MODEL // 2
FOLD = 64
FROW = 96
BIG = 1.0e30
LOW = -3.0e38
TAKEN = -3.4e38
ROUNDS = TOPK // 8
IDX_SCALE = HEAD ** -0.5 * N_IDX ** -0.5
LAST_TILE_N = 2 * P

W_STAGE = 4
FIRST = 4
GROUP = 2
N_GROUP = KC // GROUP
GATE_PAIR = PAIRS - 2


def n_keys(i):
    return (i + 1) * P


def n_cols(i):
    return max(LAST_TILE_N, n_keys(i))


def score_at(i):
    return sum(n_keys(j) for j in range(1, i))


def plan_ring():
    ring = []
    for t in range(N_TILES):
        ring.append(("w", t))
        if t >= T_PAIR + 4 * GATE_PAIR:
            ring.append(("g", t - T_PAIR - 4 * GATE_PAIR))
    return ring + [("o", u) for u in range(N_WO)]


RING = plan_ring()
RING_AT = {item: e for e, item in enumerate(RING)}


def split_no(item):
    return item[1] if item[0] == "w" else N_TILES + item[1]


def build(nc, small_rows, x, w_mod, b_gate, w_tiles, b_forget, w_out, final_gain, out):
    ctx = ExitStack()
    with ctx:
        plan = {"at": 16512}

        def sb(name, shape, dt=F32, at=None):
            size = 4
            for n in shape[1:]:
                size *= n
            if at is None:
                at = plan["at"]
                plan["at"] += (size + 31) // 32 * 32
            t = nc.alloc_sbuf_tensor_at(name, shape, dt, offset=at)
            return t, at, size

        def sem(name):
            return ctx.enter_context(nc.semaphore(name))

        h_hi, a_hhi, _ = sb("h_hi", [P, KC, SEQ], F32R)
        h_lo, a_hlo, _ = sb("h_lo", [P, KC, SEQ], F32R)
        wo0_hi, _, _ = sb("wo0_hi", [P, PAIRS, HALF], F32R, at=a_hhi)
        wo0_lo, _, _ = sb("wo0_lo", [P, PAIRS, HALF], F32R, at=a_hlo)
        qk, a_qk, _ = sb("qk", [P, 2, 2, 4, SEQ], F32R)
        x_in, _, _ = sb("x_in", [P, QT, D_MODEL], F32, at=a_qk)
        x_norm, _, _ = sb("x_norm", [P, QT, D_MODEL], F32, at=a_qk + 4 * QT * D_MODEL)
        wo1_hi, _, _ = sb("wo1_hi", [P, PAIRS, HALF], F32R, at=a_qk)
        wo1_lo, _, _ = sb("wo1_lo", [P, PAIRS, HALF], F32R, at=a_qk + 4 * PAIRS * HALF)
        pt_hi, a_pt, s_pt = sb("pt_hi", [P, 2, QT, SEQ], F32R)
        pt_lo, _, _ = sb("pt_lo", [P, 2, QT, SEQ], F32R)
        mod_in, _, _ = sb("mod_in", [P, 2, KC, 2, GROUP * P], F32, at=a_pt)
        sq_junk2, _, _ = sb("sq_junk2", [P, D_MODEL], F32, at=a_pt)
        ki_hi, a1, s1 = sb("ki_hi", [P, SEQ], F32R, at=a_pt)
        ki_lo, a1, s1 = sb("ki_lo", [P, SEQ], F32R, at=a1 + s1)
        kwf, a1, s1 = sb("kwf", [P, SEQ], F32, at=a1 + s1)
        relu_s, a1, s1 = sb("relu_s", [P, 2, SEQ], F32, at=a1 + s1)
        gz, a1, s1 = sb("gz", [P, SEQ], F32, at=a1 + s1)
        ga, a1, s1 = sb("ga", [P, SEQ], F32, at=a1 + s1)
        ge, a1, s1 = sb("ge", [P, SEQ], F32, at=a1 + s1)
        gl, a1, s1 = sb("gl", [P, SEQ], F32, at=a1 + s1)
        glf, a1, s1 = sb("glf", [P, SEQ], F32, at=a1 + s1)
        gcum, a1, s1 = sb("gcum", [P, SEQ], F32, at=a1 + s1)
        g_one, a1, s1 = sb("g_one", [P, SEQ], F32, at=a1 + s1)
        w_in, _, _ = sb("w_stage", [P, W_STAGE, KC, P], F32)
        w_hi, a_ws, s_ws = sb("w_hi", [P, 2, KC, P], F32R)
        w_lo, _, _ = sb("w_lo", [P, 2, KC, P], F32R)
        first_hi, _, _ = sb("first_hi", [P, FIRST, KC, P], F32R, at=a_ws)
        res, _, _ = sb("res", [P, QT, D_MODEL], F32, at=a_ws)
        vv, _, _ = sb("vv", [P, QT, 2, P], F32R)
        gg, a_gg, _ = sb("gg", [P, 2, SEQ], F32)
        fgain, _, _ = sb("fgain", [P, D_MODEL], F32, at=a_gg)
        v_t, a_vt, s1 = sb("v_t", [P, SEQ], F32)
        g_th, _, _ = sb("g_th", [P, SEQ], F32)
        gate_acc, _, _ = sb("gate_acc", [P, D_MODEL], F32)
        y_f, a_yf, _ = sb("y_f", [P, SEQ], F32)
        y_g, _, _ = sb("y_g", [P, SEQ], F32)
        mod_acc, _, _ = sb("mod_acc", [P, 2, 2, GROUP * P], F32, at=a_yf)
        y_bot, _, _ = sb("y_bot", [HEAD, SEQ], F32)
        y_hi, a_yhi, _ = sb("y_hi", [P, PAIRS, SEQ], F32R)
        y_lo, a_ylo, _ = sb("y_lo", [P, PAIRS, SEQ], F32R)
        h_f, _, _ = sb("h_f", [P, KC, SEQ], F32, at=a_yhi)
        q_idx, _, _ = sb("q_idx", [P, N_IDX, SEQ], F32R, at=a_ylo)
        first_lo, _, _ = sb("first_lo", [P, FIRST, KC, P], F32R, at=a_ylo)
        l_neg, a_l, _ = sb("l_neg", [P, 2, SEQ], F32)
        gate_sb, _, _ = sb("gate_sb", [P, D_MODEL], F32, at=a_l)
        probs, a_p, _ = sb("probs", [P, 3, SEQ], F32)
        w4_hi, _, s1 = sb("w4_hi", [P, KC, P], F32R, at=a_l)
        w4_lo, _, _ = sb("w4_lo", [P, KC, P], F32R, at=a_l + s1)
        o_tmp, _, _ = sb("o_tmp", [P, 2, SEQ], F32, at=a_p)
        sq_junk, _, _ = sb("sq_junk", [P, D_MODEL], F32, at=a_p)
        assert a_p == a_l + 2 * 4 * SEQ
        bias_t, _, _ = sb("bias_t", [P, SEQ], F32R)
        tri, _, _ = sb("tri", [P, SEQ], F32)
        score, _, _ = sb("score", [P, score_at(QT)], F32)
        ident, _, _ = sb("ident", [P, P], F32)
        ones, _, _ = sb("ones", [P, P], F32)
        rows, _, _ = sb("rows", [40, P], F32)
        cols, _, _ = sb("cols", [P, 40], F32)
        c_th, _, _ = sb("c_th", [P, KC], F32)
        c_act, _, _ = sb("c_act", [P, KC], F32)
        mod_sh, _, _ = sb("mod_sh", [P, KC], F32)
        mod_sc, _, _ = sb("mod_sc", [P, KC], F32)
        mod_a, _, _ = sb("mod_a", [P, KC], F32)
        ssq, _, _ = sb("ssq", [P, 3 * QT], F32)
        var, _, _ = sb("var", [P, 2 * QT], F32)
        rstd, _, _ = sb("rstd", [P, 2 * QT], F32)
        power, _, _ = sb("power", [P, 1], F32)
        ssq_part, _, _ = sb("ssq_part", [P, QT], F32)
        w_row, _, _ = sb("w_row", [P, QT, N_IDX], F32)
        bf_col, _, _ = sb("bf_col", [P, 1], F32)
        slope, _, _ = sb("slope", [N_HEAD - N_FOX, 1], F32)
        keyno_i, _, _ = sb("keyno_i", [N_HEAD - N_FOX, SEQ], mybir.dt.int32, at=a_gg)
        l_min, _, _ = sb("l_min", [P, 4], F32)
        p_sum, _, _ = sb("p_sum", [P, 4], F32)
        p_rec, _, _ = sb("p_rec", [P, 4], F32)
        top8, _, _ = sb("top8", [P, 8], F32)
        assert plan["at"] <= 229344, plan["at"]

        bank = [ctx.enter_context(nc.psum_tensor(f"bank{i}", [P, SEQ], F32)) for i in range(8)]
        pj = bank[0:2]
        ps = bank[2:4]
        pt = bank[4:6]
        py, px = bank[6], bank[7]

        s_small = sem("small_loaded")
        s_x = [sem(f"x_loaded{i}") for i in range(QT)]
        s_mod_in = [sem(f"mod_loaded{i}") for i in range(2 * N_GROUP)]
        s_first = [sem(f"first_weights_loaded{i}") for i in range(N_GROUP)]
        s_bf = sem("b_forget_loaded")
        s_stage = [sem(f"weights_loaded{i}") for i in range(W_STAGE)]
        s_bgate = sem("b_gate_loaded")
        s_res = [sem(f"residual_loaded{i}") for i in range(QT)]
        s_fg = sem("final_gain_loaded")
        s_ident = sem("identity_ready")
        s_const = sem("constants_ready")
        s_rows_t = sem("rows_transposed")
        s_cols = sem("columns_ready")
        s_cth = sem("c_tanh")
        s_cact = sem("c_act_ready")
        s_macc = sem("mod_accumulated")
        s_mred = sem("mod_reduced")
        s_ab = sem("mod_columns_ready")
        s_ssq = sem("square_sums")
        s_var = sem("variances")
        s_rstd = sem("rstd_ready")
        s_xn = sem("x_normalised")
        s_xt = sem("x_transposed")
        s_xe = sem("x_evacuated")
        s_hf = sem("h_ready")
        s_hhi = sem("h_hi_ready")
        s_hlo = sem("h_lo_ready")
        s_whi = sem("weights_hi")
        s_wlo = sem("weights_lo")
        s_proj = sem("tile_projected")
        s_hi = sem("tile_hi_evacuated")
        s_ev = sem("tile_evacuated")
        s_kwf = sem("tile0_copied")
        s_wt = sem("index_weights_transposed")
        s_wr = sem("index_weights_ready")
        s_fg1 = sem("forget_vector_steps")
        s_fg2 = sem("forget_scalar_steps")
        s_bias = sem("key_bias_ready")
        s_kid = sem("index_keys_doubled")
        s_is = sem("index_products")
        s_ir = sem("index_relu")
        s_ia = sem("index_accumulated")
        s_tk = sem("topk_steps")
        s_dup = [sem(f"pair_operands_doubled{i}") for i in range(2)]
        s_th = sem("g_tanh")
        s_vt = sem("v_transposed")
        s_vhi = sem("v_hi")
        s_vlo = sem("v_lo")
        s_s = sem("logits_ready")
        s_min = sem("logits_masked")
        s_exp = sem("exp_done")
        s_rec = sem("sum_inverted")
        s_pn = sem("probs_scaled")
        s_tr = sem("probs_transposed")
        s_pth = sem("probs_t_hi")
        s_ptl = sem("probs_t_lo")
        s_pv = sem("values_summed")
        s_yb = sem("y_bottom_copied")
        s_ys = sem("y_summed")
        s_yg = sem("y_gated")
        s_yhi = sem("y_hi")
        s_ylo = sem("y_lo")
        s_gz = sem("gate_acc_zeroed")
        s_ga = sem("gate_accumulated")
        s_gb = sem("gate_broadcast")
        s_gs = sem("gate_stored")
        s_o = sem("output_products")
        s_ot = sem("output_gated")
        s_or = sem("residual_added")
        s_sq2 = sem("final_square_sums")
        s_part = sem("first_half_shares")
        s_v2 = sem("final_variances")
        s_rstd2 = sem("final_rstd_ready")
        s_fgm = sem("first_half_gained")
        s_fin0 = sem("first_half_finished")
        s_fin = sem("rows_finished")
        s_out = sem("rows_stored")

        def tile_no(p, c):
            return T_PAIR + 4 * p + c

        def hi_count(t):
            return t + 1 if t < T_PAIR else T_PAIR + 2 * ((t - T_PAIR) // 4) + (t - T_PAIR) % 4 + 1

        IDX_STEPS = [(i, h) for i in range(1, QT) for h in range(N_IDX)]
        PER_M = 4 * KC * 3 // len(IDX_STEPS)
        ROUND_LIST = [(i, r) for i in range(1, QT) for r in range(ROUNDS)]
        ROUND_SLOTS = 4 * 8
        BANK_X = [0, 1, 2, 3, 4, 5, 0, 1]

        def done_tile(p, j):
            return tile_no(p, 3) + j // 2

        def tile_bank(t):
            return [pj[0], pj[1], ps[0], ps[1], pt[0]][t] if t < T_PAIR else pj[t % 2]

        def split_of(t):
            if t < FIRST:
                return first_hi[:, t, :, :], first_lo[:, t, :, :]
            if t == FIRST:
                return w4_hi[:, :, :], w4_lo[:, :, :]
            return w_hi[:, t % 2, :, :], w_lo[:, t % 2, :, :]

        def splits_before(item):
            n = split_no(item)
            return N_GROUP + n - FIRST

        O_GROUPS = [(hf, i) for hf in range(2) for i in range(QT)]
        O_EARLY = 2

        def wo_parts(hf):
            return (wo0_hi, wo0_lo) if hf == 0 else (wo1_hi, wo1_lo)

        block = ctx.enter_context(nc.Block())

        def pt_copy(act, a, n):
            i, hp = n % 4, (n // 4) % 2
            act.wait_ge(s_tr, n + 1)
            if n // 4 >= 2:
                act.wait_ge(s_pv, n // 4 - 1)
            if n == 0:
                act.wait_ge(s_const, 4 + 8 + 1 + 8 + 4 + 4)
            a.activation(pt_hi[:, hp, 0:i + 1, i * P:(i + 1) * P],
                         pt[n % 2][:, 0:n_keys(i)].rearrange("p (j q) -> p j q", q=P), ACT.Copy).then_inc(s_pth, 1)

        def y_bottom(act, a, hh):
            act.wait_ge(s_pv, hh + 1)
            if hh >= 1:
                act.wait_ge(s_ys, hh)
            a.activation(y_bot[:, :], py[HEAD:P, :], ACT.Copy).then_inc(s_yb, 1)

        def y_top(act, a, p):
            act.wait_ge(s_yg, p + 1)
            a.activation(y_hi[:, p, :], y_g[:, :], ACT.Copy).then_inc(s_yhi, 1)

        @block.sync
        def _(sp):
            sp.dma_start(rows[:, :], small_rows).then_inc(s_small, 16)
            sp.dma_start(bf_col[FROW:FROW + N_FOX, :], b_forget).then_inc(s_bf, 16)
            for i in range(QT):
                sp.dma_start(x_in[:, i, :], x[0, i * P:(i + 1) * P, :]).then_inc(s_x[i], 16)
            for gr in range(N_GROUP):
                if gr >= 2:
                    sp.wait_ge(s_macc, KC * (gr - 1))
                for half in range(2):
                    r = slice(half * KC // 2, (half + 1) * KC // 2)
                    for s in range(2):
                        c0 = s * D_MODEL + gr * GROUP * P
                        src = w_mod[0, half * D_MODEL // 2:(half + 1) * D_MODEL // 2, c0:c0 + GROUP * P]
                        sp.dma_start(mod_in[:, gr % 2, r, s, :], src.rearrange("(r p) c -> p r c", p=P))\
                            .then_inc(s_mod_in[2 * gr + half], 16)
                sp.dma_start(w_in[:, 0:FIRST, gr * GROUP:(gr + 1) * GROUP, :],
                             w_tiles[0:FIRST, :, gr * GROUP:(gr + 1) * GROUP, :].rearrange("t p k c -> p t k c"))\
                    .then_inc(s_first[gr], 16)

            def load(e):
                kind, n = RING[e]
                if e >= W_STAGE:
                    was = RING[e - W_STAGE]
                    if was[0] == "g":
                        sp.wait_ge(s_ga, was[1] + 1)
                    else:
                        sp.wait_ge(s_wlo, max(N_GROUP, splits_before(was) + 1))
                slot = w_in[:, e % W_STAGE, :, :]
                if kind == "w":
                    src = w_tiles[n]
                elif kind == "g":
                    src = w_mod[0, n * P:(n + 1) * P, 2 * D_MODEL:3 * D_MODEL]
                    slot = slot.rearrange("p k c -> p (k c)")
                else:
                    hf, u = divmod(n, N_WO // 2)
                    src = w_out[0, 2 * u * P:(2 * u + 2) * P, hf * HALF:(hf + 1) * HALF]\
                        .rearrange("(a p) n -> p a n", p=P)
                    slot = slot.rearrange("p k c -> p (k c)").rearrange("p (a n) -> p a n", a=2)
                sp.dma_start(slot, src).then_inc(s_stage[e % W_STAGE], 16)

            def copy(dst, src):
                return sp.dma_start(dst.bitcast(F32), src.bitcast(F32))

            def double(t):
                if t == 0:
                    sp.wait_ge(s_hi, 1)
                    copy(ki_hi[HEAD:P, :], ki_hi[0:HEAD, :]).then_inc(s_kid, 16)
                    sp.wait_ge(s_ev, 1)
                    copy(ki_lo[HEAD:P, :], ki_lo[0:HEAD, :]).then_inc(s_kid, 16)
                if t < T_PAIR:
                    return
                p, c = divmod(t - T_PAIR, 4)
                if c > 1:
                    return
                sp.wait_ge(s_hi, hi_count(t))
                for hd in range(2):
                    a = qk[:, p % 2, hd, :, :]
                    if c == 0:
                        copy(a[0:HEAD, 1, :], a[0:HEAD, 0, :]).then_inc(s_dup[p % 2], 16)
                    else:
                        copy(a[HEAD:P, 2, :], a[0:HEAD, 2, :]).then_inc(s_dup[p % 2], 16)
                if c == 1:
                    if p == 0:
                        sp.wait_ge(s_bias, 4)
                    if p >= 2:
                        sp.wait_ge(s_s, 8 * (p - 1))
                    for hd in range(2):
                        h = 2 * p + hd
                        top, low = (FROW + h, FOLD + h) if h < N_FOX else (h - N_FOX, 32 + h - N_FOX)
                        a = qk[:, p % 2, hd, 3, :]
                        copy(a[HEAD:HEAD + 1, :], bias_t[top:top + 1, :]).then_inc(s_dup[p % 2], 16)
                        copy(a[HEAD + 1:HEAD + 2, :], bias_t[low:low + 1, :]).then_inc(s_dup[p % 2], 16)

            doubled = 0
            for e in range(FIRST, len(RING)):
                if RING[e] == ("g", 0):
                    sp.wait_ge(s_gz, 2)
                    sp.dma_start(gate_acc[0:1, :], b_gate).then_inc(s_bgate, 16)
                load(e)
                upto = RING[e][1] - 3 if RING[e][0] == "w" and e > FIRST else \
                    N_TILES if e == RING_AT[("o", 0)] + 1 else doubled
                for t in range(doubled, upto):
                    double(t)
                doubled = max(doubled, upto)
                if RING[e] == ("o", 3):
                    sp.wait_ge(s_proj, N_TILES)
                    for i in range(QT):
                        sp.dma_start(res[:, i, :], x[0, i * P:(i + 1) * P, :]).then_inc(s_res[i], 16)
            sp.wait_ge(s_yg, PAIRS)
            sp.dma_start(fgain[:, :], final_gain.to_broadcast([P, D_MODEL])).then_inc(s_fg, 16)
            for i in range(QT):
                sp.wait_ge(s_fin0, i + 1)
                sp.dma_start(out[0, i * P:(i + 1) * P, 0:HALF], res[:, i, 0:HALF]).then_inc(s_out, 16)
                sp.wait_ge(s_fin, i + 1)
                sp.dma_start(out[0, i * P:(i + 1) * P, HALF:], res[:, i, HALF:]).then_inc(s_out, 16)
            sp.wait_ge(s_out, 2 * 16 * QT)

        @block.gpsimd
        def _(pool):
            g = nc.gpsimd
            g.memset(power[:, :], -0.5).then_inc(s_gz, 1)
            g.memset(gate_acc[:, :], 0.0).then_inc(s_gz, 1)
            g.memset(ident[:, :], 0.0).then_inc(s_ident, 1)
            g.memset(ones[:, :], 1.0).then_inc(s_const, 1)
            pool.wait_ge(s_ident, 1)
            g.affine_select(out=ident[:, :], in_=ident[:, :], compare_op=ALU.not_equal, fill=1.0, base=0,
                            pattern=[[-1, P]], channel_multiplier=1).then_inc(s_ident, 1)
            g.memset(tri[:, :], 0.0).then_inc(s_const, 1)
            pool.wait_ge(s_const, 2)
            g.affine_select(out=tri[:, SEQ - P:SEQ], in_=tri[:, SEQ - P:SEQ], compare_op=ALU.is_ge, fill=BIG,
                            base=0, pattern=[[-1, P]], channel_multiplier=1).then_inc(s_const, 1)
            g.memset(slope[:, :], 0.0).then_inc(s_const, 1)
            for h in range(N_HEAD - N_FOX):
                pool.wait_ge(s_const, 4 + h)
                g.affine_select(out=slope[:, :], in_=slope[:, :], compare_op=ALU.not_equal,
                                fill=2.0 ** -(8.0 * (h + 1) / (N_HEAD - N_FOX)), base=-h,
                                pattern=[[0, 1]], channel_multiplier=1).then_inc(s_const, 1)
            g.iota(keyno_i[:, :], pattern=[[1, SEQ]], base=0, channel_multiplier=0).then_inc(s_const, 1)
            def inv_root(i, s_from, s_to):
                pool.wait_ge(s_from, i % QT + 1)
                g.tensor_tensor(rstd[:, i:i + 1], var[:, i:i + 1], power[:, :], ALU.pow).then_inc(s_to, 1)

            pool.wait_ge(s_gz, 1)
            for i in range(QT):
                inv_root(i, s_var, s_rstd)
            pool.wait_ge(s_xt, 8)
            for par in range(2):
                for hd in range(2):
                    g.memset(qk[HEAD:P, par, hd, 1, :].bitcast(F32), 0.0).then_inc(s_const, 1)
                    g.memset(qk[HEAD:P, par, hd, 3, :].bitcast(F32), 0.0).then_inc(s_const, 1)
            pool.wait_ge(s_const, 4 + 8 + 1 + 8)
            for par in range(2):
                for hd in range(2):
                    g.memset(qk[HEAD:HEAD + 2, par, hd, 1, :].bitcast(F32), 1.0).then_inc(s_const, 1)
            pool.wait_ge(s_const, 4 + 8 + 1 + 8 + 4)

            def split_lo(item):
                e = RING_AT[item]
                pool.wait_ge(s_whi, splits_before(item) + 1)
                src = w_in[:, e % W_STAGE, :, :]
                if item[0] == "w":
                    hi, lo = split_of(item[1])
                    g.tensor_tensor(lo, src, hi.bitcast(F32), ALU.subtract).then_inc(s_wlo, 1)
                else:
                    hf, u = divmod(item[1], N_WO // 2)
                    hi, lo = wo_parts(hf)
                    src = src.rearrange("p k c -> p (k c)").rearrange("p (a n) -> p a n", a=2)
                    g.tensor_tensor(lo[:, 2 * u:2 * u + 2, :], src, hi[:, 2 * u:2 * u + 2, :].bitcast(F32),
                                    ALU.subtract).then_inc(s_wlo, 1)

            for gr in range(N_GROUP):
                pool.wait_ge(s_whi, gr + 1)
                k = slice(gr * GROUP, (gr + 1) * GROUP)
                g.tensor_tensor(first_lo[:, :, k, :], w_in[:, 0:FIRST, k, :], first_hi[:, :, k, :].bitcast(F32),
                                ALU.subtract).then_inc(s_wlo, 1)
            for t in range(FIRST, T_PAIR + 5):
                split_lo(("w", t))
            pool.wait_ge(s_ia, len(IDX_STEPS))
            pool.wait_ge(s_bias, 4)
            for par in range(2):
                g.memset(pt_hi[:, par, QT - 1, 2 * P:3 * P].bitcast(F32), 0.0).then_inc(s_const, 1)
                g.memset(pt_lo[:, par, QT - 1, 2 * P:3 * P].bitcast(F32), 0.0).then_inc(s_const, 1)

            def scale_probs(n):
                pool.wait_ge(s_rec, n + 1)
                pr = probs[:, n % 3, 0:n_keys(n % 4)]
                g.tensor_scalar(pr, pr, p_rec[:, n % 4:n % 4 + 1], 1.0, ALU.mult, ALU.mult).then_inc(s_pn, 1)

            for p in range(PAIRS):
                for j in range(8):
                    n = 8 * p + j
                    scale_probs(n)
                    if j % 2 == 0 and done_tile(p, j) + 2 < N_TILES:
                        split_lo(("w", done_tile(p, j) + 2))
                    if p == PAIRS - 1 and j < 2:
                        split_lo(("o", 2 * j))
                        split_lo(("o", 2 * j + 1))
                    if p >= 1 and j == 5:
                        pool.wait_ge(s_yhi, p)
                        g.tensor_tensor(y_lo[:, p - 1, :], y_g[:, :], y_hi[:, p - 1, :].bitcast(F32),
                                        ALU.subtract).then_inc(s_ylo, 1)
            pool.wait_ge(s_yhi, PAIRS)
            g.tensor_tensor(y_lo[:, PAIRS - 1, :], y_g[:, :], y_hi[:, PAIRS - 1, :].bitcast(F32),
                            ALU.subtract).then_inc(s_ylo, 1)
            for u in range(N_WO // 2, N_WO):
                split_lo(("o", u))
            for i in range(QT):
                inv_root(QT + i, s_v2, s_rstd2)

        @block.scalar
        def _(act):
            a = nc.scalar
            act.wait_ge(s_cols, 1)
            a.activation(c_th[:, :], cols[:, 0:KC], ACT.Tanh, scale=0.5).then_inc(s_cth, 1)
            for i in range(QT):
                act.wait_ge(s_x[i], 16)
                if i:
                    act.wait_ge(s_ssq, i)
                a.activation(sq_junk[:, :], x_in[:, i, :], ACT.Square, accum_out=ssq[:, i:i + 1]).then_inc(s_ssq, 1)
            for i in range(QT):
                for gp in range(2):
                    n = 2 * i + gp
                    act.wait_ge(s_xt, n + 1)
                    a.activation(h_f[:, 4 * gp:4 * gp + 4, i * P:(i + 1) * P],
                                 bank[BANK_X[n]][:, :].rearrange("p (k t) -> p k t", k=4), ACT.Copy)\
                        .then_inc(s_xe, 1)

            def split_hi(item):
                n, e = split_no(item), RING_AT[item]
                act.wait_ge(s_stage[e % W_STAGE], 16 * (e // W_STAGE))
                src = w_in[:, e % W_STAGE, :, :]
                if item[0] == "w":
                    if n > FIRST:
                        act.wait_ge(s_proj, max(FIRST, n - 1))
                    a.activation(split_of(n)[0], src, ACT.Copy).then_inc(s_whi, 1)
                else:
                    hf, u = divmod(item[1], N_WO // 2)
                    if hf == 0:
                        act.wait_ge(s_proj, N_TILES)
                    else:
                        act.wait_ge(s_s, 8 * PAIRS)
                    src = src.rearrange("p k c -> p (k c)").rearrange("p (a n) -> p a n", a=2)
                    a.activation(wo_parts(hf)[0][:, 2 * u:2 * u + 2, :], src, ACT.Copy).then_inc(s_whi, 1)

            def evac(t):
                src = tile_bank(t)
                if t < T_PAIR:
                    act.wait_ge(s_proj, t + 1)
                    if t == 0:
                        a.activation(kwf[:, :], src[:, :], ACT.Copy).then_inc(s_kwf, 1)
                        a.activation(ki_hi[0:HEAD, :], src[0:HEAD, :], ACT.Copy).then_inc(s_hi, 1)
                        return
                    for hd in range(2):
                        ins = a.activation(q_idx[0:HEAD, 2 * (t - T_QIDX) + hd, :],
                                           src[hd * HEAD:(hd + 1) * HEAD, :], ACT.Copy)
                    ins.then_inc(s_hi, 1)
                    return
                p, c = divmod(t - T_PAIR, 4)
                if c == 2:
                    return
                act.wait_ge(s_proj, t + 1)
                if c == 3:
                    if p:
                        act.wait_ge(s_ev, tile_no(p - 1, 3) + 1)
                    a.activation(g_th[:, :], src[:, :], ACT.Tanh, scale=0.5).then_inc(s_th, 1)
                    return
                if p == 0 and c == 0:
                    act.wait_ge(s_const, 4 + 8 + 1 + 8 + 4)
                if p >= 2:
                    act.wait_ge(s_s, 8 * (p - 1))
                for hd in range(2):
                    ins = a.activation(qk[0:HEAD, p % 2, hd, 2 * c, :], src[hd * HEAD:(hd + 1) * HEAD, :],
                                       ACT.Copy, scale=-(HEAD ** -0.5) if c == 0 else 1.0)
                ins.then_inc(s_hi, 1)

            for gr in range(N_GROUP):
                act.wait_ge(s_first[gr], 16)
                if gr == 0:
                    act.wait_ge(s_ssq, QT)
                ks = slice(gr * GROUP, (gr + 1) * GROUP)
                a.activation(first_hi[:, :, ks, :], w_in[:, 0:FIRST, ks, :], ACT.Copy).then_inc(s_whi, 1)
                for k in range(gr * GROUP, (gr + 1) * GROUP):
                    act.wait_ge(s_hf, k + 1)
                    a.activation(h_hi[:, k, :], h_f[:, k, :], ACT.Copy).then_inc(s_hhi, 1)
            split_hi(("w", FIRST))
            for t in range(T_PAIR):
                if t == 0:
                    act.wait_ge(s_proj, FIRST)
                    split_hi(("w", FIRST + 1))
                evac(t)
                if t == T_PAIR - 1:
                    split_hi(("w", FIRST + 2))
                if t == 1:
                    act.wait_ge(s_fg1, 1)
                    a.activation(ga[FROW:FROW + N_FOX, :], gz[FROW:FROW + N_FOX, :], ACT.Abs).then_inc(s_fg2, 1)
                    act.wait_ge(s_fg2, 1)
                    a.activation(ge[FROW:FROW + N_FOX, :], ga[FROW:FROW + N_FOX, :], ACT.Exp, scale=-1.0)\
                        .then_inc(s_fg2, 1)
                    act.wait_ge(s_fg2, 2)
                    a.activation(gl[FROW:FROW + N_FOX, :], ge[FROW:FROW + N_FOX, :], ACT.Ln, bias=1.0)\
                        .then_inc(s_fg2, 1)
            for m, (i, h) in enumerate(IDX_STEPS):
                act.wait_ge(s_is, m + 1)
                if m >= 2:
                    act.wait_ge(s_ia, m - 1)
                a.activation(relu_s[:, m % 2, 0:n_keys(i)], ps[m % 2][:, 0:n_keys(i)], ACT.Relu).then_inc(s_ir, 1)
                if m % 6 == 1 and m > 6:
                    split_hi(("w", tile_no(0, m // 6 - 1) + 2))
                    evac(tile_no(0, m // 6 - 1))
            for p in range(PAIRS):
                for j in range(8):
                    n, i = 8 * p + j, j % 4
                    act.wait_ge(s_min, n + 1)
                    if n >= 3:
                        act.wait_ge(s_tr, n - 2)
                    a.activation(probs[:, n % 3, 0:n_keys(i)], l_neg[:, n % 2, 0:n_keys(i)], ACT.Exp,
                                 bias=l_min[:, n % 4:n % 4 + 1], scale=-1.0,
                                 accum_out=p_sum[:, n % 4:n % 4 + 1]).then_inc(s_exp, 1)
                    if n >= 2:
                        pt_copy(act, a, n - 2)
                    if j == 3 and p >= 1:
                        y_bottom(act, a, 2 * p - 1)
                    if j == 7:
                        y_bottom(act, a, 2 * p)
                    if j == 0:
                        evac(tile_no(p, 3))
                    if j in (2, 4) and p < PAIRS - 1:
                        evac(tile_no(p + 1, j // 2 - 1))
                    if j == 4:
                        act.wait_ge(s_vt, p + 1)
                        if p >= 1:
                            act.wait_ge(s_pv, 2 * p)
                        a.activation(vv[:, :, :, 0:HEAD],
                                     px[:, :].rearrange("p (j h d) -> p j h d", j=QT, h=2), ACT.Copy)\
                            .then_inc(s_vhi, 1)
                        if p >= 1:
                            y_top(act, a, p - 1)
                    if j % 2 == 0 and done_tile(p, j) + 2 < N_TILES:
                        split_hi(("w", done_tile(p, j) + 2))
                    if p == PAIRS - 1 and j < 2:
                        split_hi(("o", 2 * j))
                        split_hi(("o", 2 * j + 1))
            pt_copy(act, a, 8 * PAIRS - 2)
            pt_copy(act, a, 8 * PAIRS - 1)
            y_bottom(act, a, 2 * PAIRS - 1)
            y_top(act, a, PAIRS - 1)
            for u in range(N_WO // 2, N_WO):
                split_hi(("o", u))
            for n, (hf, i) in enumerate(O_GROUPS):
                act.wait_ge(s_or, n + 1)
                if n:
                    act.wait_ge(s_sq2, n)
                a.activation(sq_junk2[:, 0:HALF], res[:, i, hf * HALF:(hf + 1) * HALF], ACT.Square,
                             accum_out=ssq[:, QT + n:QT + n + 1]).then_inc(s_sq2, 1)
                if hf == 1:
                    act.wait_ge(s_rstd2, i + 1)
                    act.wait_ge(s_fgm, i + 1)
                    a.activation(res[:, i, 0:HALF], res[:, i, 0:HALF], ACT.Copy,
                                 scale=rstd[:, QT + i:QT + i + 1]).then_inc(s_fin0, 1)

        @block.vector
        def _(dve):
            v = nc.vector
            dve.wait_ge(s_rows_t, 1)
            v.tensor_copy(cols[:, :], py[:, 0:40]).then_inc(s_cols, 1)
            dve.wait_ge(s_cols, 1)
            dve.wait_ge(s_cth, 1)
            v.tensor_scalar(c_th[:, :], c_th[:, :], 0.5, 0.5, ALU.mult, ALU.add).then_inc(s_cact, 1)
            dve.wait_ge(s_cact, 1)
            v.tensor_tensor(c_act[:, :], c_th[:, :], cols[:, 0:KC], ALU.mult).then_inc(s_cact, 1)
            dve.wait_ge(s_cact, 2)

            for i in range(QT):
                dve.wait_ge(s_ssq, i + 1)
                v.tensor_scalar(var[:, i:i + 1], ssq[:, i:i + 1], 1.0 / D_MODEL, EPS, ALU.mult, ALU.add)\
                    .then_inc(s_var, 1)
            for i in range(QT):
                dve.wait_ge(s_rstd, i + 1)
                v.tensor_scalar(x_norm[:, i, :], x_in[:, i, :], rstd[:, i:i + 1], None, ALU.mult).then_inc(s_xn, 1)

            for gr in range(N_GROUP):
                acc = mod_acc[:, gr % 2, :, :]
                for k in range(KC):
                    n = KC * gr + k
                    dve.wait_ge(s_mod_in[2 * gr + k // (KC // 2)], 32)
                    if k == 0:
                        if gr >= 2:
                            dve.wait_ge(s_mred, gr - 1)
                        v.tensor_scalar(acc, mod_in[:, gr % 2, 0, :, :], c_act[:, 0:1], None, ALU.mult)\
                            .then_inc(s_macc, 1)
                    else:
                        dve.wait_ge(s_macc, n)
                        v.scalar_tensor_tensor(out=acc, in0=mod_in[:, gr % 2, k, :, :], scalar=c_act[:, k:k + 1],
                                               in1=acc, op0=ALU.mult, op1=ALU.add).then_inc(s_macc, 1)
                ks = slice(gr * GROUP, (gr + 1) * GROUP)
                bias_of = [cols[:, (2 + s) * KC + gr * GROUP:(2 + s) * KC + (gr + 1) * GROUP] for s in range(2)]
                dve.wait_ge(s_mred, gr + 1)
                at_x = 2 * GROUP * gr
                v.tensor_tensor(mod_sh[:, ks], px[:, at_x:at_x + GROUP], bias_of[0], ALU.add).then_inc(s_ab, 1)
                v.tensor_tensor(mod_sc[:, ks], px[:, at_x + GROUP:at_x + 2 * GROUP], bias_of[1], ALU.add)\
                    .then_inc(s_ab, 1)
                dve.wait_ge(s_ab, 3 * gr + 2)
                v.scalar_tensor_tensor(out=mod_a[:, ks], in0=mod_sc[:, ks], scalar=1.0,
                                       in1=cols[:, KC + gr * GROUP:KC + (gr + 1) * GROUP],
                                       op0=ALU.add, op1=ALU.mult).then_inc(s_ab, 1)
                dve.wait_ge(s_ab, 3 * gr + 3)
                if gr == 0:
                    dve.wait_ge(s_xe, 2 * QT)
                for k in range(gr * GROUP, (gr + 1) * GROUP):
                    v.tensor_scalar(h_f[:, k, :], h_f[:, k, :], mod_a[:, k:k + 1], mod_sh[:, k:k + 1],
                                    ALU.mult, ALU.add).then_inc(s_hf, 1)
                for k in range(gr * GROUP, (gr + 1) * GROUP):
                    dve.wait_ge(s_hhi, k + 1)
                    v.tensor_tensor(h_lo[:, k, :], h_f[:, k, :], h_hi[:, k, :].bitcast(F32),
                                    ALU.subtract).then_inc(s_hlo, 1)
            dve.wait_ge(s_const, 4 + 8 + 1)
            v.tensor_scalar(bias_t[0:N_HEAD - N_FOX, :], keyno_i[:, :], slope[:, 0:1], -1.0, ALU.mult, ALU.mult)\
                .then_inc(s_bias, 1)
            v.memset(bias_t[32:32 + N_HEAD - N_FOX, :].bitcast(F32), 0.0).then_inc(s_bias, 1)

            def evac(t):
                src = tile_bank(t)
                if t < T_PAIR:
                    dve.wait_ge(s_hi, hi_count(t))
                    if t == 0:
                        v.tensor_tensor(ki_lo[0:HEAD, :], src[0:HEAD, :], ki_hi[0:HEAD, :].bitcast(F32),
                                        ALU.subtract).then_inc(s_ev, 1)
                        return
                    for hd in range(2):
                        q = q_idx[:, 2 * (t - T_QIDX) + hd, :]
                        ins = v.tensor_tensor(q[HEAD:P, :], src[hd * HEAD:(hd + 1) * HEAD, :],
                                              q[0:HEAD, :].bitcast(F32), ALU.subtract)
                    ins.then_inc(s_ev, 1)
                    return
                p, c = divmod(t - T_PAIR, 4)
                if c == 2:
                    dve.wait_ge(s_proj, t + 1)
                    if p:
                        dve.wait_ge(s_vt, p)
                    v.tensor_copy(v_t[:, :], src[:, :]).then_inc(s_ev, 1)
                    return
                if c == 3:
                    dve.wait_ge(s_th, p + 1)
                    if p >= 2:
                        dve.wait_ge(s_yg, p - 1)
                    v.scalar_tensor_tensor(out=gg[:, p % 2, :], in0=g_th[:, :], scalar=1.0, in1=src[:, :],
                                           op0=ALU.add, op1=ALU.mult).then_inc(s_ev, 1)
                    return
                dve.wait_ge(s_hi, hi_count(t))
                for hd in range(2):
                    o = qk[:, p % 2, hd, :, :]
                    part = src[hd * HEAD:(hd + 1) * HEAD, :]
                    if c == 0:
                        ins = v.scalar_tensor_tensor(out=o[HEAD:P, 0, :], in0=part, scalar=-(HEAD ** -0.5),
                                                     in1=o[0:HEAD, 0, :].bitcast(F32),
                                                     op0=ALU.mult, op1=ALU.subtract)
                    else:
                        ins = v.tensor_tensor(o[0:HEAD, 3, :], part, o[0:HEAD, 2, :].bitcast(F32), ALU.subtract)
                ins.then_inc(s_ev, 1)

            F = slice(FROW, FROW + N_FOX)
            for t in range(T_PAIR):
                evac(t)
                if t == 0:
                    dve.wait_ge(s_kwf, 1)
                    dve.wait_ge(s_bf, 16)
                    v.tensor_scalar(gz[F, :], kwf[F, :], bf_col[F, 0:1], None, ALU.add).then_inc(s_fg1, 1)
                if t == 2:
                    dve.wait_ge(s_fg2, 3)
                    v.scalar_tensor_tensor(out=glf[F, :], in0=gz[F, :], scalar=0.0, in1=gl[F, :],
                                           op0=ALU.min, op1=ALU.subtract).then_inc(s_fg1, 1)
                    v.memset(g_one[F, :], 1.0).then_inc(s_fg1, 1)
                    dve.wait_ge(s_fg1, 3)
                    v.tensor_tensor_scan(gcum[F, :], g_one[F, :], glf[F, :], 0.0, ALU.mult, ALU.add)\
                        .then_inc(s_fg1, 1)
                    dve.wait_ge(s_fg1, 4)
                    v.tensor_copy(bias_t[F, :], gcum[F, :]).then_inc(s_bias, 1)
                    dve.wait_ge(s_bias, 3)
                    v.tensor_tensor(bias_t[FOLD:FOLD + N_FOX, :], gcum[F, :], bias_t[F, :].bitcast(F32),
                                    ALU.subtract).then_inc(s_bias, 1)
                if t == 3:
                    dve.wait_ge(s_wt, 1)
                    v.tensor_scalar(w_row[:, :, :],
                                    px[:, :].rearrange("p (i f) -> p i f", i=QT)[:, :, FOLD:FOLD + N_IDX],
                                    IDX_SCALE, None, ALU.mult).then_inc(s_wr, 1)
                    dve.wait_ge(s_wr, 1)
            for m, (i, h) in enumerate(IDX_STEPS):
                sc = score[:, score_at(i):score_at(i) + n_keys(i)]
                dve.wait_ge(s_ir, m + 1)
                rl = relu_s[:, m % 2, 0:n_keys(i)]
                if h == 0:
                    v.tensor_scalar(sc, rl, w_row[:, i, 0:1], None, ALU.mult).then_inc(s_ia, 1)
                else:
                    dve.wait_ge(s_ia, m)
                    v.scalar_tensor_tensor(out=sc, in0=rl, scalar=w_row[:, i, h:h + 1], in1=sc,
                                           op0=ALU.mult, op1=ALU.add).then_inc(s_ia, 1)
                if h == N_IDX - 1:
                    diag = score[:, score_at(i) + i * P:score_at(i) + n_keys(i)]
                    dve.wait_ge(s_ia, m + 1)
                    v.scalar_tensor_tensor(out=diag, in0=tri[:, SEQ - P:SEQ], scalar=LOW / BIG, in1=diag,
                                           op0=ALU.mult, op1=ALU.add).then_inc(s_tk, 1)
                if m % 6 == 1 and m > 6:
                    evac(tile_no(0, m // 6 - 1))

            tk = [QT - 1]

            def topk_round(i, r):
                sc = score[:, score_at(i):score_at(i) + n_keys(i)]
                dve.wait_ge(s_tk, tk[0])
                v.max(top8[:, :], sc).then_inc(s_tk, 1)
                dve.wait_ge(s_tk, tk[0] + 1)
                v.match_replace(sc, top8[:, :], sc, TAKEN).then_inc(s_tk, 1)
                tk[0] += 2
                if r == ROUNDS - 1:
                    dve.wait_ge(s_tk, tk[0])
                    v.tensor_scalar(sc, sc, (LOW + TAKEN) / 2, BIG, ALU.is_gt, ALU.mult).then_inc(s_tk, 1)
                    tk[0] += 1

            def invert_sum(n):
                dve.wait_ge(s_exp, n + 1)
                v.reciprocal(p_rec[:, n % 4:n % 4 + 1], p_sum[:, n % 4:n % 4 + 1]).then_inc(s_rec, 1)

            def pt_low(n):
                i, hp = n % 4, (n // 4) % 2
                dve.wait_ge(s_pth, n + 1)
                hi = pt_hi[:, hp, 0:i + 1, i * P:(i + 1) * P].bitcast(F32)
                v.tensor_tensor(pt_lo[:, hp, 0:i + 1, i * P:(i + 1) * P],
                                pt[n % 2][:, 0:n_keys(i)].rearrange("p (j q) -> p j q", q=P), hi,
                                ALU.subtract).then_inc(s_ptl, 1)

            def y_sum(hh):
                dve.wait_ge(s_yb, hh + 1)
                if hh >= 2 and hh % 2 == 0:
                    dve.wait_ge(s_yg, hh // 2)
                v.tensor_tensor(y_f[hh % 2 * HEAD:(hh % 2 + 1) * HEAD, :], py[0:HEAD, :], y_bot[:, :], ALU.add)\
                    .then_inc(s_ys, 1)

            def y_gate(p):
                dve.wait_ge(s_ys, 2 * p + 2)
                if p:
                    dve.wait_ge(s_ylo, p)
                v.scalar_tensor_tensor(out=y_g[:, :], in0=y_f[:, :], scalar=0.5, in1=gg[:, p % 2, :],
                                       op0=ALU.mult, op1=ALU.mult).then_inc(s_yg, 1)

            def gate_sum(c):
                e = RING_AT[("g", c)]
                dve.wait_ge(s_stage[e % W_STAGE], 16 * (e // W_STAGE))
                if c == 0:
                    dve.wait_ge(s_bgate, 16)
                if c:
                    dve.wait_ge(s_ga, c)
                v.scalar_tensor_tensor(out=gate_acc[:, :],
                                       in0=w_in[:, e % W_STAGE, :, :].rearrange("p k c -> p (k c)"),
                                       scalar=c_act[:, c:c + 1], in1=gate_acc[:, :],
                                       op0=ALU.mult, op1=ALU.add).then_inc(s_ga, 1)

            done = 0
            for p in range(PAIRS):
                for j in range(8):
                    n, i = 8 * p + j, j % 4
                    dve.wait_ge(s_s, n + 1)
                    if n >= 2:
                        dve.wait_ge(s_exp, n - 1)
                    if n == 4 * N_FOX:
                        dve.wait_ge(s_tk, tk[0])
                    if p < PAIRS // 2 or i == 0:
                        mask = tri[:, SEQ - n_keys(i):SEQ]
                    else:
                        mask = score[:, score_at(i):score_at(i) + n_keys(i)]
                    v.tensor_tensor_reduce(l_neg[:, n % 2, 0:n_keys(i)], ps[n % 2][:, 0:n_keys(i)], mask,
                                           1.0, 3.0e38, ALU.add, ALU.min, l_min[:, n % 4:n % 4 + 1])\
                        .then_inc(s_min, 1)
                    fill = []
                    if n < ROUND_SLOTS:
                        upto = len(ROUND_LIST) * (n + 1) // ROUND_SLOTS
                        fill = ROUND_LIST[done:upto]
                        done = upto
                    for i2, r in fill[:1]:
                        topk_round(i2, r)
                    invert_sum(n)
                    for i2, r in fill[1:]:
                        topk_round(i2, r)
                    if p in (GATE_PAIR - 1, GATE_PAIR) and j % 2 == 1:
                        gate_sum(4 * (p - GATE_PAIR + 1) + j // 2)
                    if n >= 2:
                        pt_low(n - 2)
                    if j == 3 and p >= 1:
                        y_sum(2 * p - 1)
                        y_gate(p - 1)
                    if j == 7:
                        y_sum(2 * p)
                    if j == 0:
                        evac(tile_no(p, 3))
                    if j in (2, 4, 6) and p < PAIRS - 1:
                        evac(tile_no(p + 1, j // 2 - 1))
                    if j == 4:
                        dve.wait_ge(s_vhi, p + 1)
                        v.tensor_tensor(vv[:, :, :, HEAD:P],
                                        px[:, :].rearrange("p (j h d) -> p j h d", j=QT, h=2),
                                        vv[:, :, :, 0:HEAD].bitcast(F32), ALU.subtract).then_inc(s_vlo, 1)
            pt_low(8 * PAIRS - 2)
            pt_low(8 * PAIRS - 1)
            y_sum(2 * PAIRS - 1)
            y_gate(PAIRS - 1)
            for hf in range(2):
                dve.wait_ge(s_gb, hf + 1)
                if hf == 0:
                    dve.wait_ge(s_exp, 8 * PAIRS)
                v.tensor_copy(gate_sb[:, hf * HALF:(hf + 1) * HALF], pt[hf][:, :]).then_inc(s_gs, 1)
            dve.wait_ge(s_gs, 2)
            dve.wait_ge(s_fg, 16)
            for n, (hf, i) in enumerate(O_GROUPS):
                dve.wait_ge(s_o, n + 1)
                if n >= 2:
                    dve.wait_ge(s_or, n - 1)
                if n == 0:
                    dve.wait_ge(s_tr, 8 * PAIRS)
                v.tensor_tensor(o_tmp[:, n % 2, :], bank[n][:, :], gate_sb[:, hf * HALF:(hf + 1) * HALF], ALU.mult)\
                    .then_inc(s_ot, 1)
                dve.wait_ge(s_ot, n + 1)
                if hf == 0:
                    dve.wait_ge(s_res[i], 16)
                r = res[:, i, hf * HALF:(hf + 1) * HALF]
                v.tensor_tensor(r, r, o_tmp[:, n % 2, :], ALU.add).then_inc(s_or, 1)
                if hf == 0:
                    dve.wait_ge(s_sq2, n + 1)
                    v.tensor_scalar(ssq_part[:, i:i + 1], ssq[:, QT + n:QT + n + 1], 1.0 / D_MODEL, EPS,
                                    ALU.mult, ALU.add).then_inc(s_part, 1)
                    v.tensor_tensor(r, r, fgain[:, 0:HALF], ALU.mult).then_inc(s_fgm, 1)
                else:
                    dve.wait_ge(s_part, i + 1)
                    dve.wait_ge(s_sq2, n + 1)
                    v.tensor_scalar(var[:, QT + i:QT + i + 1], ssq[:, QT + n:QT + n + 1], 1.0 / D_MODEL,
                                    ssq_part[:, i:i + 1], ALU.mult, ALU.add).then_inc(s_v2, 1)
                    dve.wait_ge(s_rstd2, i + 1)
                    v.scalar_tensor_tensor(out=r, in0=r, scalar=rstd[:, QT + i:QT + i + 1],
                                           in1=fgain[:, HALF:], op0=ALU.mult, op1=ALU.mult).then_inc(s_fin, 1)

        @block.tensor
        def _(pe):
            t_ = nc.tensor
            pe.wait_ge(s_small, 16)
            pe.wait_ge(s_ident, 2)
            t_.transpose(py[:, 0:40], rows[:, :], ident[0:40, 0:40]).then_inc(s_rows_t, 1)
            for i in range(QT):
                pe.wait_ge(s_xn, i + 1)
                for gp in range(2):
                    n = 2 * i + gp
                    if n >= 6:
                        pe.wait_ge(s_xe, n - 5)
                    for k in range(4):
                        ins = t_.transpose(bank[BANK_X[n]][:, k * P:(k + 1) * P],
                                           x_norm[:, i, (4 * gp + k) * P:(4 * gp + k + 1) * P], ident[:, :])
                    ins.then_inc(s_xt, 1)
            pe.wait_ge(s_const, 1)
            pe.wait_ge(s_xe, 2 * QT)
            for gr in range(N_GROUP):
                pe.wait_ge(s_macc, KC * (gr + 1))
                if gr:
                    pe.wait_ge(s_ab, 3 * gr)
                for s in range(2):
                    for k in range(GROUP):
                        c0 = 2 * GROUP * gr + GROUP * s + k
                        ins = t_.matmul(px[:, c0:c0 + 1], mod_acc[:, gr % 2, s, k * P:(k + 1) * P],
                                        ones[:, 0:1], start=True, stop=True)
                ins.then_inc(s_mred, 1)
                pe.wait_ge(s_wlo, gr + 1)
                for k in range(gr * GROUP, (gr + 1) * GROUP):
                    pe.wait_ge(s_hlo, k + 1)
                    for t in range(FIRST):
                        hi, lo = split_of(t)
                        for n, (w, h) in enumerate(((lo, h_hi), (hi, h_lo), (hi, h_hi))):
                            ins = t_.matmul(tile_bank(t)[:, :], w[:, k, :], h[:, k, :],
                                            start=(k == 0 and n == 0), stop=(k == KC - 1 and n == 2))
                        if k == KC - 1:
                            ins.then_inc(s_proj, 1)

            def project(t, part, parts):
                steps = [(k, s) for k in range(KC) for s in range(3)]
                size = len(steps) // parts
                acc = tile_bank(t)
                hi, lo = split_of(t)
                if part == 0:
                    pe.wait_ge(s_wlo, splits_before(("w", t)) + 1)
                    if t >= T_PAIR:
                        pe.wait_ge(s_ev, t - 1 if t > T_PAIR else 2)
                for k, s in steps[part * size:(part + 1) * size]:
                    w = lo if s == 0 else hi
                    h = h_lo if s == 1 else h_hi
                    ins = t_.matmul(acc[:, :], w[:, k, :], h[:, k, :],
                                    start=(k == 0 and s == 0), stop=(k == KC - 1 and s == 2))
                if part == parts - 1:
                    ins.then_inc(s_proj, 1)

            project(FIRST, 0, 1)
            pe.wait_ge(s_kwf, 1)
            for i in range(QT):
                ins = t_.transpose(px[:, i * P:(i + 1) * P], kwf[:, i * P:(i + 1) * P], ident[:, :])
            ins.then_inc(s_wt, 1)
            for m, (i, h) in enumerate(IDX_STEPS):
                if m == 0:
                    pe.wait_ge(s_kid, 32)
                    pe.wait_ge(s_ev, T_PAIR)
                if m >= 2:
                    pe.wait_ge(s_ir, m - 1)
                q = q_idx[:, h, i * P:(i + 1) * P]
                t_.matmul(ps[m % 2][:, 0:n_keys(i)], q, ki_lo[:, 0:n_keys(i)], start=True, stop=False)
                t_.matmul(ps[m % 2][:, 0:n_keys(i)], q, ki_hi[:, 0:n_keys(i)], start=False, stop=True)\
                    .then_inc(s_is, 1)
                project(tile_no(0, m // 6), m % 6, 6)

            def transposes(n):
                i = n % 4
                pe.wait_ge(s_pn, n + 1)
                if n >= 2:
                    pe.wait_ge(s_ptl, n - 1)
                for j in range(i + 1):
                    ins = t_.transpose(pt[n % 2][:, j * P:(j + 1) * P], probs[:, n % 3, j * P:(j + 1) * P],
                                       ident[:, :])
                ins.then_inc(s_tr, 1)

            def values(hh):
                hp = hh % 2
                pe.wait_ge(s_ptl, 4 * hh + 4)
                pe.wait_ge(s_vlo, hh // 2 + 1)
                if hh:
                    pe.wait_ge(s_ys, hh)
                for j in range(QT):
                    c0 = min(j, QT - 2) * P
                    for src in (pt_lo, pt_hi):
                        ins = t_.matmul(py[:, c0:SEQ], vv[:, j, hp, :], src[:, hp, j, c0:SEQ],
                                        start=(j == 0 and src is pt_lo), stop=(j == QT - 1 and src is pt_hi))
                ins.then_inc(s_pv, 1)

            def out_part(n, pairs):
                hf, i = O_GROUPS[n]
                hi, lo = wo_parts(hf)
                for p in pairs:
                    pe.wait_ge(s_ylo, p + 1)
                    pe.wait_ge(s_wlo, splits_before(("o", hf * (N_WO // 2) + p // 2)) + 1)
                    for s in range(3):
                        y = y_lo if s == 0 else y_hi
                        w = lo if s == 1 else hi
                        ins = t_.matmul(bank[n][:, :], y[:, p, i * P:(i + 1) * P], w[:, p, :],
                                        start=(p == 0 and s == 0), stop=(p == PAIRS - 1 and s == 2))
                    if p == PAIRS - 1:
                        ins.then_inc(s_o, 1)

            for p in range(PAIRS):
                for j in range(8):
                    n, i = 8 * p + j, j % 4
                    if n == 0:
                        pe.wait_ge(s_ir, len(IDX_STEPS))
                    if j == 0:
                        pe.wait_ge(s_dup[p % 2], 128 * (p // 2 + 1))
                        pe.wait_ge(s_ev, tile_no(p, 1) + 1)
                    if n >= 2:
                        pe.wait_ge(s_min, n - 1)
                    a = qk[:, p % 2, j // 4, :, :]
                    t_.matmul(ps[n % 2][:, 0:n_cols(i)], a[0:HEAD + 32, 1, i * P:(i + 1) * P],
                              a[0:HEAD + 32, 3, 0:n_cols(i)], start=True, stop=False)
                    t_.matmul(ps[n % 2][:, 0:n_cols(i)], a[:, 0, i * P:(i + 1) * P],
                              a[:, 2, 0:n_cols(i)], start=False, stop=True).then_inc(s_s, 1)
                    if n >= 2:
                        transposes(n - 2)
                    if j == 3:
                        pe.wait_ge(s_ev, tile_no(p, 2) + 1)
                        if p:
                            pe.wait_ge(s_vlo, p)
                        for b in range(QT):
                            ins = t_.transpose(px[:, b * P:(b + 1) * P], v_t[:, b * P:(b + 1) * P], ident[:, :])
                        ins.then_inc(s_vt, 1)
                    if p < PAIRS - 1:
                        project(tile_no(p + 1, j // 2), j % 2, 2)
                    elif j >= 1:
                        if j == 1:
                            pe.wait_ge(s_ev, N_TILES)
                        for n2 in range(O_EARLY):
                            out_part(n2, [j - 1])
                    if j == 2 and p >= 1:
                        values(2 * p - 1)
                    if j == 6:
                        values(2 * p)
            transposes(8 * PAIRS - 2)
            for n2 in range(O_EARLY, QT):
                if n2 == O_EARLY:
                    pe.wait_ge(s_min, 8 * PAIRS)
                    out_part(n2, range(3))
                    transposes(8 * PAIRS - 1)
                    out_part(n2, range(3, PAIRS - 1))
                else:
                    out_part(n2, range(PAIRS - 1))
                if n2 == O_EARLY:
                    values(2 * PAIRS - 1)
            pe.wait_ge(s_ga, KC)
            pe.wait_ge(s_ptl, 8 * PAIRS)
            for hf in range(2):
                t_.matmul(pt[hf][:, :], ones[:, :], gate_acc[:, hf * HALF:(hf + 1) * HALF], start=True, stop=True)\
                    .then_inc(s_gb, 1)
            for n2 in range(QT):
                out_part(n2, [PAIRS - 1])
            pe.wait_ge(s_gs, 2)
            pe.wait_ge(s_ys, 2 * PAIRS)
            for n2 in range(QT, 2 * QT):
                out_part(n2, range(PAIRS))


_SMALL = (2 + 3) * D_MODEL // P


def kernel(x, c, w_mod, b_mod, norm_gain, w_in, b_forget, w_out, final_gain):
    import concourse.bacc as bacc
    from concourse.bass_utils import run_bass_kernel_spmd

    widths = [N_FOX * HEAD] * 3 + [N_FOX, N_FOX * HEAD] + [512] * 3 + [N_IDX * HEAD, HEAD, N_IDX, 512]
    at = np.concatenate([[0], np.cumsum(widths)])
    q_a, k_a, v_a, f_g, g_a, q_b, k_b, v_b, q_i, k_i, w_i, g_b = (slice(at[n], at[n + 1]) for n in range(12))
    w = np.asarray(w_in)[0]
    first = np.zeros((D_MODEL, P), w.dtype)
    first[:, 0:HEAD] = w[:, k_i]
    first[:, FOLD:FOLD + N_IDX] = w[:, w_i]
    first[:, FROW:FROW + N_FOX] = w[:, f_g]
    order = [first] + [w[:, q_i][:, u * P:(u + 1) * P] for u in range(N_IDX // 2)]
    for p in range(PAIRS):
        u = p % (PAIRS // 2)
        for part in ((q_a, k_a, v_a, g_a) if p < PAIRS // 2 else (q_b, k_b, v_b, g_b)):
            order.append(w[:, part][:, u * P:(u + 1) * P])
    w_tiles = np.ascontiguousarray(np.stack(order).reshape(N_TILES, KC, P, P).transpose(0, 2, 1, 3))
    arrays = {
        "small_rows": np.concatenate([np.asarray(a).reshape(-1, P) for a in (c, norm_gain, b_mod)]),
        "x": np.asarray(x), "w_mod": np.asarray(w_mod),
        "b_gate": np.ascontiguousarray(np.asarray(b_mod)[:, 2 * D_MODEL:]),
        "w_tiles": w_tiles, "b_forget": np.asarray(b_forget).reshape(N_FOX, 1),
        "w_out": np.asarray(w_out), "final_gain": np.asarray(final_gain).reshape(1, D_MODEL),
    }
    nc = bacc.Bacc("TRN2", target_bir_lowering=False, num_devices=1)
    args = [nc.dram_tensor(name, a.shape, mybir.dt.from_np(a.dtype), kind="ExternalInput").ap()
            for name, a in arrays.items()]
    out = nc.dram_tensor("out", (1, SEQ, D_MODEL), F32, kind="ExternalOutput").ap()
    build(nc, *args, out)
    r = run_bass_kernel_spmd(nc, [arrays], core_ids=[0])
    return r.results[0]["out"]
```

```python
from contextlib import ExitStack

import numpy as np

import concourse.bass as bass
from concourse import mybir

ALU = mybir.AluOpType
ACT = mybir.ActivationFunctionType
F32 = mybir.dt.float32
F32R = mybir.dt.float32r

P = 128
D_MODEL = 1024
SEQ = 512
HEAD = 64
N_HEAD = 16
N_FOX = 8
N_IDX = 8
TOPK = min(256, SEQ // 4)
EPS = 1e-6
KC = D_MODEL // P
QT = SEQ // P
PAIRS = N_HEAD // 2
T_QIDX = 1
T_PAIR = 5
N_TILES = T_PAIR + 4 * PAIRS
N_WO = 8
HALF = D_MODEL // 2
FOLD = 64
FROW = 96
IDX_DEEP = 4
BIG = 1.0e30
LOW = -3.0e38
TAKEN = -3.4e38
ROUNDS = TOPK // 8
IDX_SCALE = HEAD ** -0.5 * N_IDX ** -0.5
MIN_COLS = 2 * P

W_STAGE = 4
FIRST = 4
GROUP = 2
N_GROUP = KC // GROUP
ROWS_V = KC - 2
GATE_PAIR = PAIRS - 2


def n_keys(i):
    return (i + 1) * P


def n_cols(i):
    return max(MIN_COLS, n_keys(i))


def score_at(i):
    return sum(n_keys(j) for j in range(1, i))


def plan_ring():
    ring = []
    for t in range(N_TILES):
        ring.append(("w", t))
        if t >= T_PAIR + 4 * GATE_PAIR:
            ring.append(("g", t - T_PAIR - 4 * GATE_PAIR))
    return ring + [("o", u) for u in range(N_WO)]


RING = plan_ring()
RING_AT = {item: e for e, item in enumerate(RING)}


def split_no(item):
    return item[1] if item[0] == "w" else N_TILES + item[1]


def build(nc, small_rows, x, w_mod, b_gate, w_tiles, b_forget, w_out, final_gain, out):
    ctx = ExitStack()
    with ctx:
        plan = {"at": 16512}

        def sb(name, shape, dt=F32, at=None):
            size = 4
            for n in shape[1:]:
                size *= n
            if at is None:
                at = plan["at"]
                plan["at"] += (size + 31) // 32 * 32
            t = nc.alloc_sbuf_tensor_at(name, shape, dt, offset=at)
            return t, at, size

        def sem(name):
            return ctx.enter_context(nc.semaphore(name))

        h_hi, a_hhi, _ = sb("h_hi", [P, KC, SEQ], F32R)
        h_lo, a_hlo, _ = sb("h_lo", [P, KC, SEQ], F32R)
        wo0_hi, _, _ = sb("wo0_hi", [P, PAIRS, HALF], F32R, at=a_hhi)
        wo0_lo, _, _ = sb("wo0_lo", [P, PAIRS, HALF], F32R, at=a_hlo)
        qk, a_qk, _ = sb("qk", [P, 2, 2, 4, SEQ], F32R)
        x_in, _, _ = sb("x_in", [P, QT, D_MODEL], F32, at=a_qk)
        x_norm, _, _ = sb("x_norm", [P, QT, D_MODEL], F32, at=a_qk + 4 * QT * D_MODEL)
        wo1_hi, _, _ = sb("wo1_hi", [P, PAIRS, HALF], F32R, at=a_qk)
        wo1_lo, _, _ = sb("wo1_lo", [P, PAIRS, HALF], F32R, at=a_qk + 4 * PAIRS * HALF)
        pt_hi, a_pt, s_pt = sb("pt_hi", [P, 2, QT, SEQ], F32R)
        pt_lo, _, _ = sb("pt_lo", [P, 2, QT, SEQ], F32R)
        mod_in, _, _ = sb("mod_in", [P, 2, KC, 2, GROUP * P], F32, at=a_pt)
        sq_junk2, _, _ = sb("sq_junk2", [P, D_MODEL], F32, at=a_pt)
        ki_hi, a1, s1 = sb("ki_hi", [P, SEQ], F32R, at=a_pt)
        ki_lo, a1, s1 = sb("ki_lo", [P, SEQ], F32R, at=a1 + s1)
        kwf, a1, s1 = sb("kwf", [P, SEQ], F32, at=a1 + s1)
        relu_s, a1, s1 = sb("relu_s", [P, IDX_DEEP, SEQ], F32, at=a1 + s1)
        gz, a1, s1 = sb("gz", [P, SEQ], F32, at=a1 + s1)
        ga, a1, s1 = sb("ga", [P, SEQ], F32, at=a1 + s1)
        ge, a1, s1 = sb("ge", [P, SEQ], F32, at=a1 + s1)
        gl, a1, s1 = sb("gl", [P, SEQ], F32, at=a1 + s1)
        glf, a1, s1 = sb("glf", [P, SEQ], F32, at=a1 + s1)
        gcum, a1, s1 = sb("gcum", [P, SEQ], F32, at=a1 + s1)
        g_one, a1, s1 = sb("g_one", [P, SEQ], F32, at=a1 + s1)
        w_in, _, _ = sb("w_stage", [P, W_STAGE, KC, P], F32)
        w_hi, a_ws, s_ws = sb("w_hi", [P, 2, KC, P], F32R)
        w_lo, _, _ = sb("w_lo", [P, 2, KC, P], F32R)
        first_hi, _, _ = sb("first_hi", [P, FIRST, KC, P], F32R, at=a_ws)
        res, _, _ = sb("res", [P, QT, D_MODEL], F32, at=a_ws)
        vv, _, _ = sb("vv", [P, QT, 2, P], F32R)
        gg, a_gg, _ = sb("gg", [P, 2, SEQ], F32)
        fgain, _, _ = sb("fgain", [P, D_MODEL], F32, at=a_gg)
        v_t, a_vt, s1 = sb("v_t", [P, SEQ], F32)
        g_th, _, _ = sb("g_th", [P, SEQ], F32)
        gate_acc, _, _ = sb("gate_acc", [P, D_MODEL], F32)
        y_f, a_yf, _ = sb("y_f", [P, SEQ], F32)
        y_g, _, _ = sb("y_g", [P, SEQ], F32)
        mod_acc, _, _ = sb("mod_acc", [P, 2, 2, GROUP * P], F32, at=a_yf)
        mod_acc2, _, _ = sb("mod_acc2", [P, 2, 2, GROUP * P], F32, at=a_vt)
        y_bot, _, _ = sb("y_bot", [HEAD, SEQ], F32)
        y_hi, a_yhi, _ = sb("y_hi", [P, PAIRS, SEQ], F32R)
        y_lo, a_ylo, _ = sb("y_lo", [P, PAIRS, SEQ], F32R)
        h_f, _, _ = sb("h_f", [P, KC, SEQ], F32, at=a_yhi)
        q_idx, _, _ = sb("q_idx", [P, N_IDX, SEQ], F32R, at=a_ylo)
        first_lo, _, _ = sb("first_lo", [P, FIRST, KC, P], F32R, at=a_ylo)
        l_neg, a_l, _ = sb("l_neg", [P, 2, SEQ], F32)
        gate_sb, _, _ = sb("gate_sb", [P, D_MODEL], F32, at=a_l)
        probs, a_p, _ = sb("probs", [P, 3, SEQ], F32)
        w4_hi, _, s1 = sb("w4_hi", [P, KC, P], F32R, at=a_l)
        w4_lo, _, _ = sb("w4_lo", [P, KC, P], F32R, at=a_l + s1)
        o_tmp, _, _ = sb("o_tmp", [P, 2, SEQ], F32, at=a_p)
        sq_junk, _, _ = sb("sq_junk", [P, D_MODEL], F32, at=a_p)
        assert a_p == a_l + 2 * 4 * SEQ
        bias_t, _, _ = sb("bias_t", [P, SEQ], F32R)
        tri, _, _ = sb("tri", [P, SEQ], F32)
        score, _, _ = sb("score", [P, score_at(QT)], F32)
        ident, _, _ = sb("ident", [P, P], F32)
        ones, _, _ = sb("ones", [P, P], F32)
        rows, _, _ = sb("rows", [40, P], F32)
        cols, _, _ = sb("cols", [P, 40], F32)
        c_th, _, _ = sb("c_th", [P, KC], F32)
        c_act, _, _ = sb("c_act", [P, KC], F32)
        mod_sh, _, _ = sb("mod_sh", [P, KC], F32)
        mod_sc, _, _ = sb("mod_sc", [P, KC], F32)
        mod_a, _, _ = sb("mod_a", [P, KC], F32)
        ssq, _, _ = sb("ssq", [P, 3 * QT], F32)
        var, _, _ = sb("var", [P, 2 * QT], F32)
        rstd, _, _ = sb("rstd", [P, 2 * QT], F32)
        power, _, _ = sb("power", [P, 1], F32)
        ssq_part, _, _ = sb("ssq_part", [P, QT], F32)
        w_row, _, _ = sb("w_row", [P, QT, N_IDX], F32)
        bf_col, _, _ = sb("bf_col", [P, 1], F32)
        slope, _, _ = sb("slope", [N_HEAD - N_FOX, 1], F32)
        keyno_i, _, _ = sb("keyno_i", [N_HEAD - N_FOX, SEQ], mybir.dt.int32, at=a_gg)
        l_min, _, _ = sb("l_min", [P, 4], F32)
        p_sum, _, _ = sb("p_sum", [P, 4], F32)
        p_rec, _, _ = sb("p_rec", [P, 4], F32)
        top8, _, _ = sb("top8", [P, 8], F32)
        assert plan["at"] <= 229344, plan["at"]

        bank = [ctx.enter_context(nc.psum_tensor(f"bank{i}", [P, SEQ], F32)) for i in range(8)]
        pj = bank[0:2]
        ps = bank[2:4]
        pt = bank[4:6]
        py, px = bank[6], bank[7]
        p_idx = [bank[2], bank[3], bank[5], bank[6]]

        s_small = sem("small_loaded")
        s_x = [sem(f"x_loaded{i}") for i in range(QT)]
        s_mod_in = [sem(f"mod_loaded{i}") for i in range(2 * N_GROUP)]
        s_first = [sem(f"first_weights_loaded{i}") for i in range(N_GROUP)]
        s_bf = sem("b_forget_loaded")
        s_stage = [sem(f"weights_loaded{i}") for i in range(W_STAGE)]
        s_bgate = sem("b_gate_loaded")
        s_res = [sem(f"residual_loaded{i}") for i in range(QT)]
        s_fg = sem("final_gain_loaded")
        s_ident = sem("identity_ready")
        s_const = sem("constants_ready")
        s_rows_t = sem("rows_transposed")
        s_cols = sem("columns_ready")
        s_cth = sem("c_tanh")
        s_cact = sem("c_act_ready")
        s_macc = sem("mod_accumulated")
        s_macc2 = sem("mod_accumulated_by_gpsimd")
        s_mred = sem("mod_reduced")
        s_ab = sem("mod_columns_ready")
        s_ssq = sem("square_sums")
        s_var = sem("variances")
        s_rstd = sem("rstd_ready")
        s_xn = sem("x_normalised")
        s_xt = sem("x_transposed")
        s_xe = sem("x_evacuated")
        s_xev = sem("x_evacuated_by_vector")
        s_hf = sem("h_ready")
        s_hhi = sem("h_hi_ready")
        s_hlo = sem("h_lo_ready")
        s_whi = sem("weights_hi")
        s_wlo = sem("weights_lo")
        s_proj = sem("tile_projected")
        s_hfree = sem("h_chunks_free")
        s_hi = sem("tile_hi_evacuated")
        s_ev = sem("tile_evacuated")
        s_vst = sem("v_stored")
        s_kwf = sem("tile0_copied")
        s_wt = sem("index_weights_transposed")
        s_wr = sem("index_weights_ready")
        s_fg1 = sem("forget_vector_steps")
        s_fg2 = sem("forget_scalar_steps")
        s_bias = sem("key_bias_ready")
        s_kid = sem("index_keys_doubled")
        s_is = sem("index_products")
        s_ir = sem("index_relu")
        s_ia = sem("index_accumulated")
        s_tk = sem("topk_steps")
        s_dup = [sem(f"pair_operands_doubled{i}") for i in range(2)]
        s_th = sem("g_tanh")
        s_vt = sem("v_transposed")
        s_vhi = sem("v_hi")
        s_vlo = sem("v_lo")
        s_s = sem("logits_ready")
        s_min = sem("logits_masked")
        s_exp = sem("exp_done")
        s_rec = sem("sum_inverted")
        s_pn = sem("probs_scaled")
        s_tr = sem("probs_transposed")
        s_pth = sem("probs_t_hi")
        s_ptl = sem("probs_t_lo")
        s_pv = sem("values_summed")
        s_yb = sem("y_bottom_copied")
        s_ys = sem("y_summed")
        s_yg = sem("y_gated")
        s_yhi = sem("y_hi")
        s_ylo = sem("y_lo")
        s_gz = sem("gate_acc_zeroed")
        s_ga = sem("gate_accumulated")
        s_gb = sem("gate_broadcast")
        s_gs = sem("gate_stored")
        s_o = sem("output_products")
        s_ot = sem("output_gated")
        s_or = sem("residual_added")
        s_sq2 = sem("final_square_sums")
        s_part = sem("first_half_shares")
        s_v2 = sem("final_variances")
        s_rstd2 = sem("final_rstd_ready")
        s_fgm = sem("first_half_gained")
        s_fin0 = sem("first_half_finished")
        s_fin = sem("rows_finished")
        s_out = sem("rows_stored")

        C_ONES = 1
        C_TRI = C_ONES + 2
        C_ALIBI = C_TRI + 1 + (N_HEAD - N_FOX) + 1
        C_QK_ZERO = C_ALIBI + 2 * 4
        C_QK = C_QK_ZERO + 4
        C_PT = C_QK + 4

        def tile_no(p, c):
            return T_PAIR + 4 * p + c

        def hi_count(t):
            return t + 1 if t < T_PAIR else T_PAIR + 2 * ((t - T_PAIR) // 4) + (t - T_PAIR) % 4 + 1

        def evacuated(eng, t):
            p, c = divmod(t - T_PAIR, 4)
            if t >= T_PAIR and c == 2:
                eng.wait_ge(s_vst, p + 1)
            else:
                eng.wait_ge(s_ev, t + 1 if t < T_PAIR else T_PAIR + 3 * p + min(c, 2) + 1)

        IDX_STEPS = [(i, h) for h in range(N_IDX) for i in range(1, QT)]
        ROUND_LIST = [(i, r) for i in range(1, QT) for r in range(ROUNDS)]
        ROUND_COST = [0, 9, 12, 15]
        SPARE = [19, 25, 13, 13, 13, 19, 25, 19]
        round_slots, room, at = [], 0, 0
        for n in range(4 * N_FOX + QT - 1):
            room += SPARE[n % 8]
            took = []
            while at < len(ROUND_LIST) and (room >= ROUND_COST[ROUND_LIST[at][0]] or n == 4 * N_FOX + QT - 2):
                room -= ROUND_COST[ROUND_LIST[at][0]]
                took.append(ROUND_LIST[at])
                at += 1
            round_slots.append(took)
        BANK_X = [0, 1, 2, 3, 4, 5, 0, 1]
        X_ACT = 5

        def done_tile(p, j):
            return tile_no(p, 3) + j // 2

        def tile_bank(t):
            return [pj[0], pj[1], ps[0], ps[1], pt[0]][t] if t < T_PAIR else pj[t % 2]

        def split_of(t):
            if t < FIRST:
                return first_hi[:, t, :, :], first_lo[:, t, :, :]
            if t == FIRST:
                return w4_hi[:, :, :], w4_lo[:, :, :]
            return w_hi[:, t % 2, :, :], w_lo[:, t % 2, :, :]

        def splits_before(item):
            n = split_no(item)
            return N_GROUP + n - FIRST

        O_GROUPS = [(hf, i) for hf in range(2) for i in range(QT)]
        O_SPLIT = 8 * PAIRS - 10
        O_BANK = [1, 0, 7, 2, 3, 4, 5, 6]
        O_BESIDE = [[(0, 0), (0, 1)], [(0, 2), (0, 3)], [(1, 0), (1, 1)], [(1, 2), (1, 3)],
                    [(0, 4), (1, 4)], [(0, 5), (1, 5)], [(2, 0), (2, 1), (2, 2)], [(2, 3), (2, 4)]]

        def wo_parts(hf):
            return (wo0_hi, wo0_lo) if hf == 0 else (wo1_hi, wo1_lo)

        block = ctx.enter_context(nc.Block())

        def pt_copy(act, a, n):
            i, hp = n % 4, (n // 4) % 2
            act.wait_ge(s_tr, n + 1)
            if n // 4 >= 2:
                act.wait_ge(s_pv, n // 4 - 1)
            if n == 0:
                act.wait_ge(s_const, C_PT)
            a.activation(pt_hi[:, hp, 0:i + 1, i * P:(i + 1) * P],
                         pt[n % 2][:, 0:n_keys(i)].rearrange("p (j q) -> p j q", q=P), ACT.Copy).then_inc(s_pth, 1)

        def y_bottom(act, a, hh):
            act.wait_ge(s_pv, hh + 1)
            if hh >= 1:
                act.wait_ge(s_ys, hh)
            a.activation(y_bot[:, :], py[HEAD:P, :], ACT.Copy).then_inc(s_yb, 1)

        def y_top(act, a, p):
            act.wait_ge(s_yg, p + 1)
            a.activation(y_hi[:, p, :], y_g[:, :], ACT.Copy).then_inc(s_yhi, 1)

        def y_gate(eng, e, p):
            eng.wait_ge(s_ys, 2 * p + 2)
            eng.wait_ge(s_ev, T_PAIR + 3 * p + 3)
            if p:
                eng.wait_ge(s_ylo, p)
            e.tensor_tensor(y_g[:, :], y_f[:, :], gg[:, p % 2, :], ALU.mult).then_inc(s_yg, 1)

        @block.sync
        def _(sp):
            sp.dma_start(rows[:, :], small_rows).then_inc(s_small, 16)
            sp.dma_start(bf_col[FROW:FROW + N_FOX, :], b_forget).then_inc(s_bf, 16)

            def load_mod(gr, half):
                r = slice(half * KC // 2, (half + 1) * KC // 2)
                for s in range(2):
                    c0 = s * D_MODEL + gr * GROUP * P
                    src = w_mod[0, half * D_MODEL // 2:(half + 1) * D_MODEL // 2, c0:c0 + GROUP * P]
                    sp.dma_start(mod_in[:, gr % 2, r, s, :], src.rearrange("(r p) c -> p r c", p=P))\
                        .then_inc(s_mod_in[2 * gr + half], 16)

            load_mod(0, 0)
            for i in range(QT):
                sp.dma_start(x_in[:, i, :], x[0, i * P:(i + 1) * P, :]).then_inc(s_x[i], 16)
            load_mod(0, 1)
            for gr in range(N_GROUP):
                if gr >= 2:
                    sp.wait_ge(s_macc, ROWS_V * (gr - 1))
                    sp.wait_ge(s_macc2, 3 * (gr - 1))
                if gr:
                    load_mod(gr, 0)
                    load_mod(gr, 1)
                sp.dma_start(w_in[:, 0:FIRST, gr * GROUP:(gr + 1) * GROUP, :],
                             w_tiles[0:FIRST, :, gr * GROUP:(gr + 1) * GROUP, :].rearrange("t p k c -> p t k c"))\
                    .then_inc(s_first[gr], 16)

            def load(e):
                kind, n = RING[e]
                if e >= W_STAGE:
                    was = RING[e - W_STAGE]
                    if was[0] == "g":
                        sp.wait_ge(s_ga, was[1] + 1)
                    else:
                        sp.wait_ge(s_wlo, max(N_GROUP, splits_before(was) + 1))
                slot = w_in[:, e % W_STAGE, :, :]
                if kind == "w":
                    src = w_tiles[n]
                elif kind == "g":
                    src = w_mod[0, n * P:(n + 1) * P, 2 * D_MODEL:3 * D_MODEL]
                    slot = slot.rearrange("p k c -> p (k c)")
                else:
                    hf, u = divmod(n, N_WO // 2)
                    src = w_out[0, 2 * u * P:(2 * u + 2) * P, hf * HALF:(hf + 1) * HALF]\
                        .rearrange("(a p) n -> p a n", p=P)
                    slot = slot.rearrange("p k c -> p (k c)").rearrange("p (a n) -> p a n", a=2)
                sp.dma_start(slot, src).then_inc(s_stage[e % W_STAGE], 16)

            def copy(dst, src):
                return sp.dma_start(dst.bitcast(F32), src.bitcast(F32))

            def double(t):
                if t == 0:
                    sp.wait_ge(s_hi, 1)
                    copy(ki_hi[HEAD:P, :], ki_hi[0:HEAD, :]).then_inc(s_kid, 16)
                    sp.wait_ge(s_ev, 1)
                    copy(ki_lo[HEAD:P, :], ki_lo[0:HEAD, :]).then_inc(s_kid, 16)
                if t < T_PAIR:
                    return
                p, c = divmod(t - T_PAIR, 4)
                if c > 1:
                    return
                sp.wait_ge(s_hi, hi_count(t))
                for hd in range(2):
                    a = qk[:, p % 2, hd, :, :]
                    if c == 0:
                        copy(a[0:HEAD, 1, :], a[0:HEAD, 0, :]).then_inc(s_dup[p % 2], 16)
                    else:
                        copy(a[HEAD:P, 2, :], a[0:HEAD, 2, :]).then_inc(s_dup[p % 2], 16)
                if c == 1:
                    if p == 0:
                        sp.wait_ge(s_bias, 4)
                    if p >= 2:
                        sp.wait_ge(s_s, 8 * (p - 1))
                    for hd in range(2):
                        h = 2 * p + hd
                        top, low = (FROW + h, FOLD + h) if h < N_FOX else (h - N_FOX, 32 + h - N_FOX)
                        a = qk[:, p % 2, hd, 3, :]
                        copy(a[HEAD:HEAD + 1, :], bias_t[top:top + 1, :]).then_inc(s_dup[p % 2], 16)
                        copy(a[HEAD + 1:HEAD + 2, :], bias_t[low:low + 1, :]).then_inc(s_dup[p % 2], 16)

            doubled = 0
            for e in range(FIRST, len(RING)):
                if RING[e] == ("g", 0):
                    sp.wait_ge(s_gz, 2)
                    sp.dma_start(gate_acc[0:1, :], b_gate).then_inc(s_bgate, 16)
                load(e)
                upto = RING[e][1] - 3 if RING[e][0] == "w" and e > FIRST else \
                    N_TILES if e == RING_AT[("o", 0)] else doubled
                for t in range(doubled, upto):
                    double(t)
                doubled = max(doubled, upto)
                if RING[e] == ("o", 3):
                    sp.wait_ge(s_proj, N_TILES)
                    for i in range(QT):
                        sp.dma_start(res[:, i, :], x[0, i * P:(i + 1) * P, :]).then_inc(s_res[i], 16)
            sp.wait_ge(s_yg, PAIRS)
            sp.dma_start(fgain[:, :], final_gain.to_broadcast([P, D_MODEL])).then_inc(s_fg, 16)
            for i in range(QT):
                sp.wait_ge(s_fin0, i + 1)
                sp.dma_start(out[0, i * P:(i + 1) * P, 0:HALF], res[:, i, 0:HALF]).then_inc(s_out, 16)
                sp.wait_ge(s_fin, i + 1)
                sp.dma_start(out[0, i * P:(i + 1) * P, HALF:], res[:, i, HALF:]).then_inc(s_out, 16)
            sp.wait_ge(s_out, 2 * 16 * QT)

        @block.gpsimd
        def _(pool):
            g = nc.gpsimd
            g.memset(power[:, :], -0.5).then_inc(s_gz, 1)
            g.memset(gate_acc[:, :], 0.0).then_inc(s_gz, 1)
            g.memset(ident[:, :], 0.0).then_inc(s_ident, 1)
            g.memset(ones[:, :], 1.0).then_inc(s_const, 1)
            pool.wait_ge(s_ident, 1)
            g.affine_select(out=ident[:, :], in_=ident[:, :], compare_op=ALU.not_equal, fill=1.0, base=0,
                            pattern=[[-1, P]], channel_multiplier=1).then_inc(s_ident, 1)
            g.memset(tri[:, :], 0.0).then_inc(s_const, 1)
            pool.wait_ge(s_const, C_ONES + 1)
            g.affine_select(out=tri[:, SEQ - P:SEQ], in_=tri[:, SEQ - P:SEQ], compare_op=ALU.is_ge, fill=BIG,
                            base=0, pattern=[[-1, P]], channel_multiplier=1).then_inc(s_const, 1)
            g.memset(slope[:, :], 0.0).then_inc(s_const, 1)
            for h in range(N_HEAD - N_FOX):
                pool.wait_ge(s_const, C_TRI + 1 + h)
                g.affine_select(out=slope[:, :], in_=slope[:, :], compare_op=ALU.not_equal,
                                fill=2.0 ** -(8.0 * (h + 1) / (N_HEAD - N_FOX)), base=-h,
                                pattern=[[0, 1]], channel_multiplier=1).then_inc(s_const, 1)
            g.iota(keyno_i[:, :], pattern=[[1, SEQ]], base=0, channel_multiplier=0).then_inc(s_const, 1)
            def inv_root(i, s_from, s_to):
                pool.wait_ge(s_from, i % QT + 1)
                g.tensor_tensor(rstd[:, i:i + 1], var[:, i:i + 1], power[:, :], ALU.pow).then_inc(s_to, 1)

            def mod_sum(gr):
                acc = mod_acc2[:, gr % 2, :, :]
                pool.wait_ge(s_mod_in[2 * gr + 1], 32)
                if gr == 0:
                    pool.wait_ge(s_cact, 2)
                if gr >= 2:
                    pool.wait_ge(s_mred, gr - 1)
                last = mod_in[:, gr % 2, KC - 1, :, :]
                g.tensor_scalar(acc, mod_in[:, gr % 2, ROWS_V, :, :], c_act[:, ROWS_V:ROWS_V + 1], 1.0,
                                ALU.mult, ALU.mult).then_inc(s_macc2, 1)
                g.tensor_scalar(last, last, c_act[:, KC - 1:KC], 1.0, ALU.mult, ALU.mult).then_inc(s_macc2, 1)
                pool.wait_ge(s_macc2, 3 * gr + 2)
                g.tensor_tensor(acc, acc, last, ALU.add).then_inc(s_macc2, 1)

            pool.wait_ge(s_gz, 1)
            for i in range(QT):
                inv_root(i, s_var, s_rstd)
            mod_sum(0)
            def split_lo(item):
                e = RING_AT[item]
                pool.wait_ge(s_whi, splits_before(item) + 1)
                src = w_in[:, e % W_STAGE, :, :]
                if item[0] == "w":
                    hi, lo = split_of(item[1])
                    g.tensor_tensor(lo, src, hi.bitcast(F32), ALU.subtract).then_inc(s_wlo, 1)
                else:
                    hf, u = divmod(item[1], N_WO // 2)
                    hi, lo = wo_parts(hf)
                    src = src.rearrange("p k c -> p (k c)").rearrange("p (a n) -> p a n", a=2)
                    g.tensor_tensor(lo[:, 2 * u:2 * u + 2, :], src, hi[:, 2 * u:2 * u + 2, :].bitcast(F32),
                                    ALU.subtract).then_inc(s_wlo, 1)

            for gr in range(N_GROUP):
                pool.wait_ge(s_whi, gr + 1)
                k = slice(gr * GROUP, (gr + 1) * GROUP)
                g.tensor_tensor(first_lo[:, :, k, :], w_in[:, 0:FIRST, k, :], first_hi[:, :, k, :].bitcast(F32),
                                ALU.subtract).then_inc(s_wlo, 1)
                if gr + 1 < N_GROUP:
                    mod_sum(gr + 1)
            pool.wait_ge(s_xt, 8)
            pool.wait_ge(s_wlo, N_GROUP)
            for par in range(2):
                for hd in range(2):
                    g.memset(qk[HEAD:P, par, hd, 1, :].bitcast(F32), 0.0).then_inc(s_const, 1)
                    g.memset(qk[HEAD:P, par, hd, 3, :].bitcast(F32), 0.0).then_inc(s_const, 1)
            pool.wait_ge(s_const, C_QK_ZERO)
            for par in range(2):
                for hd in range(2):
                    g.memset(qk[HEAD:HEAD + 2, par, hd, 1, :].bitcast(F32), 1.0).then_inc(s_const, 1)
            pool.wait_ge(s_const, C_QK)

            for t in range(FIRST, T_PAIR + 5):
                split_lo(("w", t))
            pool.wait_ge(s_ia, len(IDX_STEPS))
            pool.wait_ge(s_bias, 4)
            for par in range(2):
                g.memset(pt_hi[:, par, QT - 1, 2 * P:3 * P].bitcast(F32), 0.0).then_inc(s_const, 1)
                g.memset(pt_lo[:, par, QT - 1, 2 * P:3 * P].bitcast(F32), 0.0).then_inc(s_const, 1)

            def scale_probs(n):
                pool.wait_ge(s_rec, n + 1)
                pr = probs[:, n % 3, 0:n_keys(n % 4)]
                g.tensor_scalar(pr, pr, p_rec[:, n % 4:n % 4 + 1], 0.5, ALU.mult, ALU.mult).then_inc(s_pn, 1)

            for p in range(PAIRS):
                for j in range(8):
                    n = 8 * p + j
                    scale_probs(n)
                    if j % 2 == 0 and done_tile(p, j) + 2 < N_TILES:
                        split_lo(("w", done_tile(p, j) + 2))
                    if O_SPLIT <= n < O_SPLIT + N_WO // 2:
                        split_lo(("o", n - O_SPLIT))
                    if p >= 1 and j == 3:
                        y_gate(pool, g, p - 1)
                    if p >= 1 and j == 5:
                        pool.wait_ge(s_yhi, p)
                        g.tensor_tensor(y_lo[:, p - 1, :], y_g[:, :], y_hi[:, p - 1, :].bitcast(F32),
                                        ALU.subtract).then_inc(s_ylo, 1)
            pool.wait_ge(s_yhi, PAIRS)
            g.tensor_tensor(y_lo[:, PAIRS - 1, :], y_g[:, :], y_hi[:, PAIRS - 1, :].bitcast(F32),
                            ALU.subtract).then_inc(s_ylo, 1)
            for u in range(N_WO // 2, N_WO):
                split_lo(("o", u))
            for i in range(QT):
                inv_root(QT + i, s_v2, s_rstd2)

        @block.scalar
        def _(act):
            a = nc.scalar
            act.wait_ge(s_cols, 1)
            a.activation(c_th[:, :], cols[:, 0:KC], ACT.Tanh, scale=0.5).then_inc(s_cth, 1)
            for i in range(QT):
                act.wait_ge(s_x[i], 16)
                if i:
                    act.wait_ge(s_ssq, i)
                a.activation(sq_junk[:, :], x_in[:, i, :], ACT.Square, accum_out=ssq[:, i:i + 1]).then_inc(s_ssq, 1)
            for i in range(QT):
                for gp in range(2):
                    n = 2 * i + gp
                    if n >= X_ACT:
                        continue
                    act.wait_ge(s_xt, n + 1)
                    a.activation(h_f[:, 4 * gp:4 * gp + 4, i * P:(i + 1) * P],
                                 bank[BANK_X[n]][:, :].rearrange("p (k t) -> p k t", k=4), ACT.Copy)\
                        .then_inc(s_xe, 1)

            def split_hi(item):
                n, e = split_no(item), RING_AT[item]
                act.wait_ge(s_stage[e % W_STAGE], 16 * (e // W_STAGE))
                src = w_in[:, e % W_STAGE, :, :]
                if item[0] == "w":
                    if n > FIRST:
                        act.wait_ge(s_proj, max(FIRST, n - 1))
                    a.activation(split_of(n)[0], src, ACT.Copy).then_inc(s_whi, 1)
                else:
                    hf, u = divmod(item[1], N_WO // 2)
                    if hf == 0 and u < N_WO // 2 - 1:
                        act.wait_ge(s_hfree, u + 1)
                    elif hf == 0:
                        act.wait_ge(s_proj, N_TILES)
                    else:
                        act.wait_ge(s_s, 8 * PAIRS)
                    src = src.rearrange("p k c -> p (k c)").rearrange("p (a n) -> p a n", a=2)
                    a.activation(wo_parts(hf)[0][:, 2 * u:2 * u + 2, :], src, ACT.Copy).then_inc(s_whi, 1)

            def evac(t):
                src = tile_bank(t)
                if t < T_PAIR:
                    act.wait_ge(s_proj, t + 1)
                    if t == 0:
                        a.activation(kwf[:, :], src[:, :], ACT.Copy).then_inc(s_kwf, 1)
                        a.activation(ki_hi[0:HEAD, :], src[0:HEAD, :], ACT.Copy).then_inc(s_hi, 1)
                        return
                    for hd in range(2):
                        ins = a.activation(q_idx[0:HEAD, 2 * (t - T_QIDX) + hd, :],
                                           src[hd * HEAD:(hd + 1) * HEAD, :], ACT.Copy)
                    ins.then_inc(s_hi, 1)
                    return
                p, c = divmod(t - T_PAIR, 4)
                act.wait_ge(s_proj, t + 1)
                if c == 2:
                    if p:
                        act.wait_ge(s_vt, p)
                    a.activation(v_t[:, :], src[:, :], ACT.Copy).then_inc(s_vst, 1)
                    return
                if c == 3:
                    if p:
                        evacuated(act, tile_no(p - 1, 3))
                    a.activation(g_th[:, :], src[:, :], ACT.Tanh, scale=0.5).then_inc(s_th, 1)
                    return
                if p == 0 and c == 0:
                    act.wait_ge(s_const, C_QK)
                if p >= 2:
                    act.wait_ge(s_s, 8 * (p - 1))
                for hd in range(2):
                    ins = a.activation(qk[0:HEAD, p % 2, hd, 2 * c, :], src[hd * HEAD:(hd + 1) * HEAD, :],
                                       ACT.Copy, scale=-(HEAD ** -0.5) if c == 0 else 1.0)
                ins.then_inc(s_hi, 1)

            for gr in range(N_GROUP):
                act.wait_ge(s_first[gr], 16)
                if gr == 0:
                    act.wait_ge(s_ssq, QT)
                ks = slice(gr * GROUP, (gr + 1) * GROUP)
                a.activation(first_hi[:, :, ks, :], w_in[:, 0:FIRST, ks, :], ACT.Copy).then_inc(s_whi, 1)
                for k in range(gr * GROUP, (gr + 1) * GROUP):
                    act.wait_ge(s_hf, k + 1)
                    a.activation(h_hi[:, k, :], h_f[:, k, :], ACT.Copy).then_inc(s_hhi, 1)
            split_hi(("w", FIRST))
            for t in range(T_PAIR):
                if t == 0:
                    act.wait_ge(s_proj, FIRST)
                    split_hi(("w", FIRST + 1))
                evac(t)
                if t == 2:
                    split_hi(("w", FIRST + 2))
                if t == 1:
                    act.wait_ge(s_fg1, 1)
                    a.activation(ga[FROW:FROW + N_FOX, :], gz[FROW:FROW + N_FOX, :], ACT.Abs).then_inc(s_fg2, 1)
                    act.wait_ge(s_fg2, 1)
                    a.activation(ge[FROW:FROW + N_FOX, :], ga[FROW:FROW + N_FOX, :], ACT.Exp, scale=-1.0)\
                        .then_inc(s_fg2, 1)
                    act.wait_ge(s_fg2, 2)
                    a.activation(gl[FROW:FROW + N_FOX, :], ge[FROW:FROW + N_FOX, :], ACT.Ln, bias=1.0)\
                        .then_inc(s_fg2, 1)
            evac(T_PAIR)
            split_hi(("w", T_PAIR + 2))
            for m, (i, h) in enumerate(IDX_STEPS):
                act.wait_ge(s_is, m + 1)
                if m >= IDX_DEEP:
                    act.wait_ge(s_ia, m - IDX_DEEP + 1)
                a.activation(relu_s[:, m % IDX_DEEP, 0:n_keys(i)], p_idx[m % IDX_DEEP][:, 0:n_keys(i)],
                             ACT.Relu).then_inc(s_ir, 1)
                if m in (1, 13):
                    evac(T_PAIR + 1 + m // 12)
                    split_hi(("w", T_PAIR + 3 + m // 12))
            for p in range(PAIRS):
                for j in range(8):
                    n, i = 8 * p + j, j % 4
                    act.wait_ge(s_min, n + 1)
                    if n >= 3:
                        act.wait_ge(s_tr, n - 2)
                    a.activation(probs[:, n % 3, 0:n_keys(i)], l_neg[:, n % 2, 0:n_keys(i)], ACT.Exp,
                                 bias=l_min[:, n % 4:n % 4 + 1], scale=-1.0,
                                 accum_out=p_sum[:, n % 4:n % 4 + 1]).then_inc(s_exp, 1)
                    if n >= 2:
                        pt_copy(act, a, n - 2)
                    if j == 3 and p >= 1:
                        y_bottom(act, a, 2 * p - 1)
                    if j == 7:
                        y_bottom(act, a, 2 * p)
                    if j == 0:
                        evac(tile_no(p, 3))
                    if j in (2, 4, 6) and p < PAIRS - 1:
                        evac(tile_no(p + 1, j // 2 - 1))
                    if j == 5 and p >= 1:
                        y_top(act, a, p - 1)
                    if j == (5 if p < PAIRS - 1 else 4):
                        act.wait_ge(s_vt, p + 1)
                        if p >= 1:
                            act.wait_ge(s_pv, 2 * p)
                        a.activation(vv[:, :, :, 0:HEAD],
                                     px[:, :].rearrange("p (j h d) -> p j h d", j=QT, h=2), ACT.Copy)\
                            .then_inc(s_vhi, 1)
                    if j % 2 == 0 and done_tile(p, j) + 2 < N_TILES:
                        split_hi(("w", done_tile(p, j) + 2))
                    if O_SPLIT <= n < O_SPLIT + N_WO // 2:
                        split_hi(("o", n - O_SPLIT))
            pt_copy(act, a, 8 * PAIRS - 2)
            pt_copy(act, a, 8 * PAIRS - 1)
            y_bottom(act, a, 2 * PAIRS - 1)
            y_top(act, a, PAIRS - 1)
            for u in range(N_WO // 2, N_WO):
                split_hi(("o", u))
            for n, (hf, i) in enumerate(O_GROUPS):
                act.wait_ge(s_or, n + 1)
                if n:
                    act.wait_ge(s_sq2, n)
                a.activation(sq_junk2[:, 0:HALF], res[:, i, hf * HALF:(hf + 1) * HALF], ACT.Square,
                             accum_out=ssq[:, QT + n:QT + n + 1]).then_inc(s_sq2, 1)
                if hf == 1:
                    act.wait_ge(s_rstd2, i + 1)
                    act.wait_ge(s_fgm, i + 1)
                    a.activation(res[:, i, 0:HALF], res[:, i, 0:HALF], ACT.Copy,
                                 scale=rstd[:, QT + i:QT + i + 1]).then_inc(s_fin0, 1)

        @block.vector
        def _(dve):
            v = nc.vector
            dve.wait_ge(s_rows_t, 1)
            v.tensor_copy(cols[:, :], py[:, 0:40]).then_inc(s_cols, 1)
            dve.wait_ge(s_cols, 1)
            dve.wait_ge(s_cth, 1)
            v.tensor_scalar(c_th[:, :], c_th[:, :], 0.5, 0.5, ALU.mult, ALU.add).then_inc(s_cact, 1)
            dve.wait_ge(s_cact, 1)
            v.tensor_tensor(c_act[:, :], c_th[:, :], cols[:, 0:KC], ALU.mult).then_inc(s_cact, 1)
            dve.wait_ge(s_cact, 2)

            def mod_sum(gr, rows_):
                acc = mod_acc[:, gr % 2, :, :]
                for k in rows_:
                    dve.wait_ge(s_mod_in[2 * gr + k // (KC // 2)], 32)
                    if k == 0:
                        if gr >= 2:
                            dve.wait_ge(s_mred, gr - 1)
                        v.tensor_scalar(acc, mod_in[:, gr % 2, 0, :, :], c_act[:, 0:1], None, ALU.mult)\
                            .then_inc(s_macc, 1)
                    else:
                        dve.wait_ge(s_macc, ROWS_V * gr + k)
                        v.scalar_tensor_tensor(out=acc, in0=mod_in[:, gr % 2, k, :, :], scalar=c_act[:, k:k + 1],
                                               in1=acc, op0=ALU.mult, op1=ALU.add).then_inc(s_macc, 1)

            mod_sum(0, range(KC // 2))
            def normalise(i):
                dve.wait_ge(s_rstd, i + 1)
                v.tensor_scalar(x_norm[:, i, :], x_in[:, i, :], rstd[:, i:i + 1], None, ALU.mult).then_inc(s_xn, 1)

            for i in range(QT):
                dve.wait_ge(s_ssq, i + 1)
                v.tensor_scalar(var[:, i:i + 1], ssq[:, i:i + 1], 1.0 / D_MODEL, EPS, ALU.mult, ALU.add)\
                    .then_inc(s_var, 1)
                if i:
                    normalise(i - 1)
            normalise(QT - 1)
            mod_sum(0, range(KC // 2, ROWS_V))
            for n in range(X_ACT, 2 * QT):
                i, gp = divmod(n, 2)
                dve.wait_ge(s_xt, n + 1)
                v.tensor_copy(h_f[:, 4 * gp:4 * gp + 4, i * P:(i + 1) * P],
                              bank[BANK_X[n]][:, :].rearrange("p (k t) -> p k t", k=4)).then_inc(s_xev, 1)

            for gr in range(N_GROUP):
                if gr == 1:
                    mod_sum(1, range(ROWS_V))
                elif gr > 1:
                    mod_sum(gr, range(ROWS_V // 2, ROWS_V))
                if 1 <= gr < N_GROUP - 1:
                    mod_sum(gr + 1, range(ROWS_V // 2))
                ks = slice(gr * GROUP, (gr + 1) * GROUP)
                bias_of = [cols[:, (2 + s) * KC + gr * GROUP:(2 + s) * KC + (gr + 1) * GROUP] for s in range(2)]
                dve.wait_ge(s_mred, gr + 1)
                at_x = 2 * GROUP * gr
                v.tensor_tensor(mod_sh[:, ks], px[:, at_x:at_x + GROUP], bias_of[0], ALU.add).then_inc(s_ab, 1)
                v.tensor_tensor(mod_sc[:, ks], px[:, at_x + GROUP:at_x + 2 * GROUP], bias_of[1], ALU.add)\
                    .then_inc(s_ab, 1)
                dve.wait_ge(s_ab, 3 * gr + 2)
                v.scalar_tensor_tensor(out=mod_a[:, ks], in0=mod_sc[:, ks], scalar=1.0,
                                       in1=cols[:, KC + gr * GROUP:KC + (gr + 1) * GROUP],
                                       op0=ALU.add, op1=ALU.mult).then_inc(s_ab, 1)
                dve.wait_ge(s_ab, 3 * gr + 3)
                if gr == 0:
                    dve.wait_ge(s_xe, X_ACT)
                    dve.wait_ge(s_xev, 2 * QT - X_ACT)
                for k in range(gr * GROUP, (gr + 1) * GROUP):
                    v.tensor_scalar(h_f[:, k, :], h_f[:, k, :], mod_a[:, k:k + 1], mod_sh[:, k:k + 1],
                                    ALU.mult, ALU.add).then_inc(s_hf, 1)
                for k in range(gr * GROUP, (gr + 1) * GROUP):
                    dve.wait_ge(s_hhi, k + 1)
                    v.tensor_tensor(h_lo[:, k, :], h_f[:, k, :], h_hi[:, k, :].bitcast(F32),
                                    ALU.subtract).then_inc(s_hlo, 1)
            dve.wait_ge(s_const, C_ALIBI)
            v.tensor_scalar(bias_t[0:N_HEAD - N_FOX, :], keyno_i[:, :], slope[:, 0:1], -1.0, ALU.mult, ALU.mult)\
                .then_inc(s_bias, 1)
            v.memset(bias_t[32:32 + N_HEAD - N_FOX, :].bitcast(F32), 0.0).then_inc(s_bias, 1)

            def evac(t):
                src = tile_bank(t)
                if t < T_PAIR:
                    dve.wait_ge(s_hi, hi_count(t))
                    if t == 0:
                        v.tensor_tensor(ki_lo[0:HEAD, :], src[0:HEAD, :], ki_hi[0:HEAD, :].bitcast(F32),
                                        ALU.subtract).then_inc(s_ev, 1)
                        return
                    for hd in range(2):
                        q = q_idx[:, 2 * (t - T_QIDX) + hd, :]
                        ins = v.tensor_tensor(q[HEAD:P, :], src[hd * HEAD:(hd + 1) * HEAD, :],
                                              q[0:HEAD, :].bitcast(F32), ALU.subtract)
                    ins.then_inc(s_ev, 1)
                    return
                p, c = divmod(t - T_PAIR, 4)
                if c == 3:
                    dve.wait_ge(s_th, p + 1)
                    if p >= 2:
                        dve.wait_ge(s_yg, p - 1)
                    v.scalar_tensor_tensor(out=gg[:, p % 2, :], in0=g_th[:, :], scalar=1.0, in1=src[:, :],
                                           op0=ALU.add, op1=ALU.mult).then_inc(s_ev, 1)
                    return
                dve.wait_ge(s_hi, hi_count(t))
                for hd in range(2):
                    o = qk[:, p % 2, hd, :, :]
                    part = src[hd * HEAD:(hd + 1) * HEAD, :]
                    if c == 0:
                        ins = v.scalar_tensor_tensor(out=o[HEAD:P, 0, :], in0=part, scalar=-(HEAD ** -0.5),
                                                     in1=o[0:HEAD, 0, :].bitcast(F32),
                                                     op0=ALU.mult, op1=ALU.subtract)
                    else:
                        ins = v.tensor_tensor(o[0:HEAD, 3, :], part, o[0:HEAD, 2, :].bitcast(F32), ALU.subtract)
                ins.then_inc(s_ev, 1)

            F = slice(FROW, FROW + N_FOX)
            for t in range(T_PAIR):
                evac(t)
                if t == 0:
                    dve.wait_ge(s_kwf, 1)
                    dve.wait_ge(s_bf, 16)
                    v.tensor_scalar(gz[F, :], kwf[F, :], bf_col[F, 0:1], None, ALU.add).then_inc(s_fg1, 1)
                if t == 2:
                    dve.wait_ge(s_fg2, 3)
                    v.scalar_tensor_tensor(out=glf[F, :], in0=gz[F, :], scalar=0.0, in1=gl[F, :],
                                           op0=ALU.min, op1=ALU.subtract).then_inc(s_fg1, 1)
                    v.memset(g_one[F, :], 1.0).then_inc(s_fg1, 1)
                    dve.wait_ge(s_fg1, 3)
                    v.tensor_tensor_scan(gcum[F, :], g_one[F, :], glf[F, :], 0.0, ALU.mult, ALU.add)\
                        .then_inc(s_fg1, 1)
                    dve.wait_ge(s_fg1, 4)
                    v.tensor_copy(bias_t[F, :], gcum[F, :]).then_inc(s_bias, 1)
                    dve.wait_ge(s_bias, 3)
                    v.tensor_tensor(bias_t[FOLD:FOLD + N_FOX, :], gcum[F, :], bias_t[F, :].bitcast(F32),
                                    ALU.subtract).then_inc(s_bias, 1)
                if t == 3:
                    dve.wait_ge(s_wt, 1)
                    v.tensor_scalar(w_row[:, :, :],
                                    px[:, :].rearrange("p (i f) -> p i f", i=QT)[:, :, FOLD:FOLD + N_IDX],
                                    IDX_SCALE, None, ALU.mult).then_inc(s_wr, 1)
                    dve.wait_ge(s_wr, 1)
            evac(T_PAIR)
            for m, (i, h) in enumerate(IDX_STEPS):
                sc = score[:, score_at(i):score_at(i) + n_keys(i)]
                dve.wait_ge(s_ir, m + 1)
                rl = relu_s[:, m % IDX_DEEP, 0:n_keys(i)]
                if h == 0:
                    v.tensor_scalar(sc, rl, w_row[:, i, 0:1], None, ALU.mult).then_inc(s_ia, 1)
                else:
                    dve.wait_ge(s_ia, m - 2)
                    v.scalar_tensor_tensor(out=sc, in0=rl, scalar=w_row[:, i, h:h + 1], in1=sc,
                                           op0=ALU.mult, op1=ALU.add).then_inc(s_ia, 1)
                if m == 1:
                    evac(T_PAIR + 1)

            for i in range(1, QT):
                diag = score[:, score_at(i) + i * P:score_at(i) + n_keys(i)]
                dve.wait_ge(s_ia, len(IDX_STEPS) - QT + 1 + i)
                v.scalar_tensor_tensor(out=diag, in0=tri[:, SEQ - P:SEQ], scalar=LOW / BIG, in1=diag,
                                       op0=ALU.mult, op1=ALU.add).then_inc(s_tk, 1)

            tk = [QT - 1]
            mask_at = {}

            def topk_round(i, r):
                sc = score[:, score_at(i):score_at(i) + n_keys(i)]
                dve.wait_ge(s_tk, tk[0])
                v.max(top8[:, :], sc).then_inc(s_tk, 1)
                dve.wait_ge(s_tk, tk[0] + 1)
                v.match_replace(sc, top8[:, :], sc, TAKEN).then_inc(s_tk, 1)
                tk[0] += 2
                if r == ROUNDS - 1:
                    dve.wait_ge(s_tk, tk[0])
                    v.tensor_scalar(sc, sc, (LOW + TAKEN) / 2, BIG, ALU.is_gt, ALU.mult).then_inc(s_tk, 1)
                    tk[0] += 1
                    mask_at[i] = tk[0]

            def invert_sum(n):
                dve.wait_ge(s_exp, n + 1)
                v.reciprocal(p_rec[:, n % 4:n % 4 + 1], p_sum[:, n % 4:n % 4 + 1]).then_inc(s_rec, 1)

            def pt_low(n):
                i, hp = n % 4, (n // 4) % 2
                dve.wait_ge(s_pth, n + 1)
                hi = pt_hi[:, hp, 0:i + 1, i * P:(i + 1) * P].bitcast(F32)
                v.tensor_tensor(pt_lo[:, hp, 0:i + 1, i * P:(i + 1) * P],
                                pt[n % 2][:, 0:n_keys(i)].rearrange("p (j q) -> p j q", q=P), hi,
                                ALU.subtract).then_inc(s_ptl, 1)

            def y_sum(hh):
                dve.wait_ge(s_yb, hh + 1)
                if hh >= 2 and hh % 2 == 0:
                    dve.wait_ge(s_yg, hh // 2)
                v.tensor_tensor(y_f[hh % 2 * HEAD:(hh % 2 + 1) * HEAD, :], py[0:HEAD, :], y_bot[:, :], ALU.add)\
                    .then_inc(s_ys, 1)

            def gate_sum(c):
                e = RING_AT[("g", c)]
                dve.wait_ge(s_stage[e % W_STAGE], 16 * (e // W_STAGE))
                if c == 0:
                    dve.wait_ge(s_bgate, 16)
                if c:
                    dve.wait_ge(s_ga, c)
                v.scalar_tensor_tensor(out=gate_acc[:, :],
                                       in0=w_in[:, e % W_STAGE, :, :].rearrange("p k c -> p (k c)"),
                                       scalar=c_act[:, c:c + 1], in1=gate_acc[:, :],
                                       op0=ALU.mult, op1=ALU.add).then_inc(s_ga, 1)

            for p in range(PAIRS):
                for j in range(8):
                    n, i = 8 * p + j, j % 4
                    dve.wait_ge(s_s, n + 1)
                    if n >= 2:
                        dve.wait_ge(s_exp, n - 1)
                    if n in range(4 * N_FOX + 1, 4 * N_FOX + QT):
                        dve.wait_ge(s_tk, mask_at[i])
                    if p < PAIRS // 2 or i == 0:
                        mask = tri[:, SEQ - n_keys(i):SEQ]
                    else:
                        mask = score[:, score_at(i):score_at(i) + n_keys(i)]
                    v.tensor_tensor_reduce(l_neg[:, n % 2, 0:n_keys(i)], ps[n % 2][:, 0:n_keys(i)], mask,
                                           1.0, 3.0e38, ALU.add, ALU.min, l_min[:, n % 4:n % 4 + 1])\
                        .then_inc(s_min, 1)
                    fill = round_slots[n] if n < len(round_slots) else []
                    for i2, r in fill[:1]:
                        topk_round(i2, r)
                    invert_sum(n)
                    for i2, r in fill[1:]:
                        topk_round(i2, r)
                    if p in (GATE_PAIR - 1, GATE_PAIR) and j % 2 == 1:
                        gate_sum(4 * (p - GATE_PAIR + 1) + j // 2)
                    if n >= 2:
                        pt_low(n - 2)
                    if j == 3 and p >= 1:
                        y_sum(2 * p - 1)
                    if j == 7:
                        y_sum(2 * p)
                    if j == 0:
                        evac(tile_no(p, 3))
                    if j in (2, 4) and p < PAIRS - 1:
                        evac(tile_no(p + 1, j // 2 - 1))
                    if j == (5 if p < PAIRS - 1 else 4):
                        dve.wait_ge(s_vhi, p + 1)
                        v.tensor_tensor(vv[:, :, :, HEAD:P],
                                        px[:, :].rearrange("p (j h d) -> p j h d", j=QT, h=2),
                                        vv[:, :, :, 0:HEAD].bitcast(F32), ALU.subtract).then_inc(s_vlo, 1)
            pt_low(8 * PAIRS - 2)
            pt_low(8 * PAIRS - 1)
            y_sum(2 * PAIRS - 1)
            y_gate(dve, v, PAIRS - 1)
            for hf in range(2):
                dve.wait_ge(s_gb, hf + 1)
                if hf == 0:
                    dve.wait_ge(s_exp, 8 * PAIRS)
                v.tensor_copy(gate_sb[:, hf * HALF:(hf + 1) * HALF], pt[hf][:, :]).then_inc(s_gs, 1)
            dve.wait_ge(s_gs, 2)
            dve.wait_ge(s_fg, 16)
            for n, (hf, i) in enumerate(O_GROUPS):
                dve.wait_ge(s_o, n + 1)
                if n >= 2:
                    dve.wait_ge(s_or, n - 1)
                if n == 0:
                    dve.wait_ge(s_tr, 8 * PAIRS)
                v.tensor_tensor(o_tmp[:, n % 2, :], bank[O_BANK[n]][:, :],
                                gate_sb[:, hf * HALF:(hf + 1) * HALF], ALU.mult).then_inc(s_ot, 1)
                dve.wait_ge(s_ot, n + 1)
                if hf == 0:
                    dve.wait_ge(s_res[i], 16)
                r = res[:, i, hf * HALF:(hf + 1) * HALF]
                v.tensor_tensor(r, r, o_tmp[:, n % 2, :], ALU.add).then_inc(s_or, 1)
                if hf == 0:
                    dve.wait_ge(s_sq2, n + 1)
                    v.tensor_scalar(ssq_part[:, i:i + 1], ssq[:, QT + n:QT + n + 1], 1.0 / D_MODEL, EPS,
                                    ALU.mult, ALU.add).then_inc(s_part, 1)
                    v.tensor_tensor(r, r, fgain[:, 0:HALF], ALU.mult).then_inc(s_fgm, 1)
                else:
                    dve.wait_ge(s_part, i + 1)
                    dve.wait_ge(s_sq2, n + 1)
                    v.tensor_scalar(var[:, QT + i:QT + i + 1], ssq[:, QT + n:QT + n + 1], 1.0 / D_MODEL,
                                    ssq_part[:, i:i + 1], ALU.mult, ALU.add).then_inc(s_v2, 1)
                    dve.wait_ge(s_rstd2, i + 1)
                    v.scalar_tensor_tensor(out=r, in0=r, scalar=rstd[:, QT + i:QT + i + 1],
                                           in1=fgain[:, HALF:], op0=ALU.mult, op1=ALU.mult).then_inc(s_fin, 1)

        @block.tensor
        def _(pe):
            t_ = nc.tensor
            pe.wait_ge(s_small, 16)
            pe.wait_ge(s_ident, 2)
            t_.transpose(py[:, 0:40], rows[:, :], ident[0:40, 0:40]).then_inc(s_rows_t, 1)
            for i in range(QT):
                pe.wait_ge(s_xn, i + 1)
                for gp in range(2):
                    n = 2 * i + gp
                    if n >= 6:
                        pe.wait_ge(s_xe, n - 5)
                    for k in range(4):
                        ins = t_.transpose(bank[BANK_X[n]][:, k * P:(k + 1) * P],
                                           x_norm[:, i, (4 * gp + k) * P:(4 * gp + k + 1) * P], ident[:, :])
                    ins.then_inc(s_xt, 1)
            pe.wait_ge(s_const, C_ONES)

            def reduce_mod(gr):
                pe.wait_ge(s_macc, ROWS_V * (gr + 1))
                pe.wait_ge(s_macc2, 3 * (gr + 1))
                if gr:
                    pe.wait_ge(s_ab, 3 * gr)
                for s in range(2):
                    for k in range(GROUP):
                        c0 = 2 * GROUP * gr + GROUP * s + k
                        for a in (mod_acc, mod_acc2):
                            ins = t_.matmul(px[:, c0:c0 + 1], a[:, gr % 2, s, k * P:(k + 1) * P],
                                            ones[:, 0:1], start=(a is mod_acc), stop=(a is mod_acc2))
                ins.then_inc(s_mred, 1)

            reduce_mod(0)
            pe.wait_ge(s_xe, X_ACT)
            pe.wait_ge(s_xev, 2 * QT - X_ACT)
            for gr in range(N_GROUP):
                pe.wait_ge(s_wlo, gr + 1)
                for k in range(gr * GROUP, (gr + 1) * GROUP):
                    pe.wait_ge(s_hlo, k + 1)
                    for t in range(FIRST):
                        hi, lo = split_of(t)
                        for n, (w, h) in enumerate(((lo, h_hi), (hi, h_lo), (hi, h_hi))):
                            ins = t_.matmul(tile_bank(t)[:, :], w[:, k, :], h[:, k, :],
                                            start=(k == 0 and n == 0), stop=(k == KC - 1 and n == 2))
                        if k == KC - 1:
                            ins.then_inc(s_proj, 1)
                    if k == gr * GROUP and gr + 1 < N_GROUP:
                        reduce_mod(gr + 1)

            def project(t, part, parts):
                steps = [(k, s) for k in range(KC) for s in range(3)]
                size = len(steps) // parts
                acc = tile_bank(t)
                hi, lo = split_of(t)
                if part == 0:
                    pe.wait_ge(s_wlo, splits_before(("w", t)) + 1)
                    if t >= T_PAIR:
                        evacuated(pe, t - 2 if t >= T_PAIR + 2 else 1)
                for k, s in steps[part * size:(part + 1) * size]:
                    w = lo if s == 0 else hi
                    h = h_lo if s == 1 else h_hi
                    ins = t_.matmul(acc[:, :], w[:, k, :], h[:, k, :],
                                    start=(k == 0 and s == 0), stop=(k == KC - 1 and s == 2))
                    if t == N_TILES - 1 and s == 2 and k % 2 == 1 and k < KC - 1:
                        ins.then_inc(s_hfree, 1)
                if part == parts - 1:
                    ins.then_inc(s_proj, 1)

            project(FIRST, 0, 1)
            project(T_PAIR, 0, 1)
            pe.wait_ge(s_kwf, 1)
            for i in range(QT):
                ins = t_.transpose(px[:, i * P:(i + 1) * P], kwf[:, i * P:(i + 1) * P], ident[:, :])
            ins.then_inc(s_wt, 1)
            project(T_PAIR + 1, 0, 1)
            for m, (i, h) in enumerate(IDX_STEPS):
                if m == 0:
                    pe.wait_ge(s_kid, 32)
                    pe.wait_ge(s_ev, T_PAIR)
                if m >= IDX_DEEP:
                    pe.wait_ge(s_ir, m - IDX_DEEP + 1)
                q = q_idx[:, h, i * P:(i + 1) * P]
                t_.matmul(p_idx[m % IDX_DEEP][:, 0:n_keys(i)], q, ki_lo[:, 0:n_keys(i)], start=True, stop=False)
                t_.matmul(p_idx[m % IDX_DEEP][:, 0:n_keys(i)], q, ki_hi[:, 0:n_keys(i)], start=False, stop=True)\
                    .then_inc(s_is, 1)
                project(T_PAIR + 2 + m // 12, m % 12, 12)

            def transposes(n):
                i = n % 4
                pe.wait_ge(s_pn, n + 1)
                if n >= 2:
                    pe.wait_ge(s_ptl, n - 1)
                for j in range(i + 1):
                    ins = t_.transpose(pt[n % 2][:, j * P:(j + 1) * P], probs[:, n % 3, j * P:(j + 1) * P],
                                       ident[:, :])
                ins.then_inc(s_tr, 1)

            def values(hh):
                hp = hh % 2
                pe.wait_ge(s_ptl, 4 * hh + 4)
                pe.wait_ge(s_vlo, hh // 2 + 1)
                if hh:
                    pe.wait_ge(s_ys, hh)
                for j in range(QT):
                    c0 = min(j, QT - 2) * P
                    for src in (pt_lo, pt_hi):
                        ins = t_.matmul(py[:, c0:SEQ], vv[:, j, hp, :], src[:, hp, j, c0:SEQ],
                                        start=(j == 0 and src is pt_lo), stop=(j == QT - 1 and src is pt_hi))
                ins.then_inc(s_pv, 1)

            def out_part(n, pairs):
                hf, i = O_GROUPS[n]
                hi, lo = wo_parts(hf)
                for p in pairs:
                    pe.wait_ge(s_ylo, p + 1)
                    pe.wait_ge(s_wlo, splits_before(("o", hf * (N_WO // 2) + p // 2)) + 1)
                    for s in range(3):
                        y = y_lo if s == 0 else y_hi
                        w = lo if s == 1 else hi
                        ins = t_.matmul(bank[O_BANK[n]][:, :], y[:, p, i * P:(i + 1) * P], w[:, p, :],
                                        start=(p == 0 and s == 0), stop=(p == PAIRS - 1 and s == 2))
                    if p == PAIRS - 1:
                        ins.then_inc(s_o, 1)

            for p in range(PAIRS):
                for j in range(8):
                    n, i = 8 * p + j, j % 4
                    if n == 0:
                        pe.wait_ge(s_ir, len(IDX_STEPS))
                    if j == 0:
                        pe.wait_ge(s_dup[p % 2], 128 * (p // 2 + 1))
                        evacuated(pe, tile_no(p, 1))
                    if n >= 2:
                        pe.wait_ge(s_min, n - 1)
                    a = qk[:, p % 2, j // 4, :, :]
                    t_.matmul(ps[n % 2][:, 0:n_cols(i)], a[0:HEAD + 32, 1, i * P:(i + 1) * P],
                              a[0:HEAD + 32, 3, 0:n_cols(i)], start=True, stop=False)
                    t_.matmul(ps[n % 2][:, 0:n_cols(i)], a[:, 0, i * P:(i + 1) * P],
                              a[:, 2, 0:n_cols(i)], start=False, stop=True).then_inc(s_s, 1)
                    if n >= 2:
                        transposes(n - 2)
                    if j == 3:
                        pe.wait_ge(s_vst, p + 1)
                        if p:
                            pe.wait_ge(s_vlo, p)
                        for b in range(QT):
                            ins = t_.transpose(px[:, b * P:(b + 1) * P], v_t[:, b * P:(b + 1) * P], ident[:, :])
                        ins.then_inc(s_vt, 1)
                    if p < PAIRS - 1:
                        project(tile_no(p + 1, j // 2), j % 2, 2)
                    else:
                        if j == 0:
                            evacuated(pe, N_TILES - 2)
                        if j == 2:
                            evacuated(pe, N_TILES - 1)
                        if j == 6:
                            pe.wait_ge(s_vlo, PAIRS)
                        for n2, p2 in O_BESIDE[j]:
                            out_part(n2, [p2])
                    if j == 2 and p >= 1:
                        values(2 * p - 1)
                    if j == 6:
                        values(2 * p)
            transposes(8 * PAIRS - 2)
            for n2 in range(2):
                out_part(n2, [PAIRS - 2])
            pe.wait_ge(s_min, 8 * PAIRS)
            out_part(3, range(2))
            transposes(8 * PAIRS - 1)
            out_part(3, range(2, 4))
            values(2 * PAIRS - 1)
            out_part(3, range(4, PAIRS - 1))
            out_part(2, range(5, PAIRS - 1))
            pe.wait_ge(s_ga, KC)
            pe.wait_ge(s_ptl, 8 * PAIRS)
            for hf in range(2):
                t_.matmul(pt[hf][:, :], ones[:, :], gate_acc[:, hf * HALF:(hf + 1) * HALF], start=True, stop=True)\
                    .then_inc(s_gb, 1)
            for n2 in range(QT):
                out_part(n2, [PAIRS - 1])
            pe.wait_ge(s_gs, 2)
            pe.wait_ge(s_ys, 2 * PAIRS)
            for p in range(PAIRS):
                for n2 in (QT, QT + 1):
                    out_part(n2, [p])
            for n2 in range(QT + 2, 2 * QT):
                out_part(n2, range(PAIRS))


def kernel(x, c, w_mod, b_mod, norm_gain, w_in, b_forget, w_out, final_gain):
    import concourse.bacc as bacc
    from concourse.bass_utils import run_bass_kernel_spmd

    widths = [N_FOX * HEAD] * 3 + [N_FOX, N_FOX * HEAD] + [512] * 3 + [N_IDX * HEAD, HEAD, N_IDX, 512]
    at = np.concatenate([[0], np.cumsum(widths)])
    q_a, k_a, v_a, f_g, g_a, q_b, k_b, v_b, q_i, k_i, w_i, g_b = (slice(at[n], at[n + 1]) for n in range(12))
    w = np.asarray(w_in)[0]
    first = np.zeros((D_MODEL, P), w.dtype)
    first[:, 0:HEAD] = w[:, k_i]
    first[:, FOLD:FOLD + N_IDX] = w[:, w_i]
    first[:, FROW:FROW + N_FOX] = w[:, f_g]
    order = [first] + [w[:, q_i][:, u * P:(u + 1) * P] for u in range(N_IDX // 2)]
    for p in range(PAIRS):
        u = p % (PAIRS // 2)
        for part in ((q_a, k_a, v_a, g_a) if p < PAIRS // 2 else (q_b, k_b, v_b, g_b)):
            order.append(w[:, part][:, u * P:(u + 1) * P])
    w_tiles = np.ascontiguousarray(np.stack(order).reshape(N_TILES, KC, P, P).transpose(0, 2, 1, 3))
    arrays = {
        "small_rows": np.concatenate([np.asarray(a).reshape(-1, P) for a in (c, norm_gain, b_mod)]),
        "x": np.asarray(x), "w_mod": np.asarray(w_mod),
        "b_gate": np.ascontiguousarray(np.asarray(b_mod)[:, 2 * D_MODEL:]),
        "w_tiles": w_tiles, "b_forget": np.asarray(b_forget).reshape(N_FOX, 1),
        "w_out": np.asarray(w_out), "final_gain": np.asarray(final_gain).reshape(1, D_MODEL),
    }
    nc = bacc.Bacc("TRN2", target_bir_lowering=False, num_devices=1)
    args = [nc.dram_tensor(name, a.shape, mybir.dt.from_np(a.dtype), kind="ExternalInput").ap()
            for name, a in arrays.items()]
    out = nc.dram_tensor("out", (1, SEQ, D_MODEL), F32, kind="ExternalOutput").ap()
    build(nc, *args, out)
    r = run_bass_kernel_spmd(nc, [arrays], core_ids=[0])
    return r.results[0]["out"]
```
